# Optimizing a Trainium2 kernel written in Bass

```python
import math, functools
import jax, jax.numpy as jnp
from jax import lax
import numpy as np

D_MODEL = 1024
BATCH = 1
SEQ = 2048
DEPTH = 1
DEC_BATCH = 8
DEC_SEQ = 4
PAST_LEN = 8192
PAGE_SIZE = 128

F32 = jnp.float32
HEAD_DIM = 64
MIX_WIDTH = D_MODEL
W_A = 3 * MIX_WIDTH // 8
W_B = MIX_WIDTH // 4
W_C = MIX_WIDTH - W_A - W_B
H_A = W_A // HEAD_DIM
H_B = W_B // HEAD_DIM
H_C = W_C // HEAD_DIM
DB = HEAD_DIM // 2
GDN_CONV = 4
GDN_CHUNK = 64
DECAY_LORA = 64
AAA_LORA = 64
GATE_LORA = 128
RWKV_GN_EPS = 64e-5
MEM_TOKENS = 256
MEM_HEADS = 4
MEM_HD = 128
MEM_INNER = MEM_HEADS * MEM_HD
D_FF = 2816
FFN_CONV = 3
Q_BLOCK = 128
NORM_EPS = 1e-6
A_COLS = 4 * W_A + 2 * H_A
B_COLS = 3 * W_B
C_COLS = 3 * W_C + DECAY_LORA + AAA_LORA + GATE_LORA
N_IN_COLS = A_COLS + B_COLS + C_COLS

kernel_name = "hymba_gdn_diffattn_rwkv7_convglu_decode_step"

def rmsnorm(x, g, eps=NORM_EPS):
    xf = x.astype(F32)
    y = xf * lax.rsqrt(jnp.mean(xf * xf, axis=-1, keepdims=True) + eps)
    return (y * g.astype(F32)).astype(x.dtype)

def causal_dwconv(x, buf, w, b=None):
    t = x.shape[1]
    width = w.shape[0]
    xp = jnp.concatenate([buf.astype(x.dtype), x], axis=1)
    y = xp[:, 0:t] * w[0]
    for j in range(1, width):
        y = y + xp[:, j:j + t] * w[j]
    if b is not None:
        y = y + b
    return y, xp[:, xp.shape[1] - (width - 1):]

def gated_delta_rule(q, k, v, beta, g, s0):
    bsz, t, h, _ = q.shape
    dv = v.shape[-1]
    c = math.gcd(t, GDN_CHUNK)
    n = t // c

    def blocks(a):
        return jnp.swapaxes(a.astype(F32).reshape((bsz, n, c) + a.shape[2:]), 2, 3)

    q, k, v, beta, g = map(blocks, (q, k, v, beta, g))
    gam = jnp.cumsum(g, axis=-1)
    diff = gam[..., :, None] - gam[..., None, :]
    strict = jnp.tril(jnp.ones((c, c), bool), -1)
    incl = jnp.tril(jnp.ones((c, c), bool))
    kb = k * beta[..., None]
    a_mat = jnp.einsum('bnhid,bnhjd->bnhij', kb, k) * jnp.exp(jnp.where(strict, diff, -jnp.inf))
    m = a_mat + jnp.eye(c, dtype=F32)
    u = lax.linalg.triangular_solve(m, v * beta[..., None], left_side=True, lower=True, unit_diagonal=True)
    w = lax.linalg.triangular_solve(m, kb * jnp.exp(gam)[..., None], left_side=True, lower=True, unit_diagonal=True)
    qk = jnp.einsum('bnhid,bnhjd->bnhij', q, k) * jnp.exp(jnp.where(incl, diff, -jnp.inf))
    q_dec = q * jnp.exp(gam)[..., None]
    k_dec = k * jnp.exp(gam[..., -1:] - gam)[..., None]
    g_last = jnp.exp(gam[..., -1])

    def step(s, xs):
        q_c, k_c, u_c, w_c, qk_c, gl = xs
        v_new = u_c - jnp.einsum('bhcd,bhde->bhce', w_c, s)
        o = jnp.einsum('bhcd,bhde->bhce', q_c, s) + jnp.einsum('bhij,bhje->bhie', qk_c, v_new)
        s = s * gl[..., None, None] + jnp.einsum('bhcd,bhce->bhde', k_c, v_new)
        return s, o

    xs = tuple(jnp.moveaxis(a, 1, 0) for a in (q_dec, k_dec, u, w, qk, g_last))
    s, o = lax.scan(step, s0.astype(F32), xs)
    o = jnp.swapaxes(jnp.moveaxis(o, 0, 1), 2, 3).reshape(bsz, t, h, dv)
    return o, s

def gdn_mixer(cols, conv_buf, s0, conv_w, a_log, dt_bias, norm_g):
    bsz, t, _ = cols.shape
    qkv_pre, z, b_logit, a_logit = jnp.split(cols, [3 * W_A, 4 * W_A, 4 * W_A + H_A], axis=-1)
    qkv, new_buf = causal_dwconv(qkv_pre, conv_buf, conv_w)
    qkv = jax.nn.silu(qkv).astype(F32)
    q, k, v = [a.reshape(bsz, t, H_A, HEAD_DIM) for a in jnp.split(qkv, 3, axis=-1)]
    q = q * lax.rsqrt(jnp.sum(q * q, axis=-1, keepdims=True) + 1e-6) * (HEAD_DIM ** -0.5)
    k = k * lax.rsqrt(jnp.sum(k * k, axis=-1, keepdims=True) + 1e-6)
    beta = jax.nn.sigmoid(b_logit.astype(F32))
    g = -jnp.exp(a_log.astype(F32)) * jax.nn.softplus(a_logit.astype(F32) + dt_bias.astype(F32))
    o, s = gated_delta_rule(q, k, v, beta, g, s0)
    o = rmsnorm(o, norm_g) * jax.nn.silu(z.astype(F32).reshape(bsz, t, H_A, HEAD_DIM))
    return o.reshape(bsz, t, W_A).astype(cols.dtype), new_buf, s.astype(cols.dtype)

def diff_lambda(lq1, lk1, lq2, lk2, lam_init):
    return (jnp.exp(jnp.sum(lq1.astype(F32) * lk1.astype(F32)))
            - jnp.exp(jnp.sum(lq2.astype(F32) * lk2.astype(F32))) + lam_init)

def diff_weights(s, lam):
    p = jax.nn.softmax(s, axis=-1)
    return p[:, :, 0] - lam * p[:, :, 1]

def diff_attn_prompt(q, k, v, lam):
    bsz, t = q.shape[:2]
    nb = t // Q_BLOCK
    kf = k.astype(F32)
    vf = v.astype(F32)
    qb = jnp.moveaxis(q.astype(F32).reshape(bsz, nb, Q_BLOCK, H_B, 2, DB), 1, 0)
    kpos = jnp.arange(t)

    def block(args):
        q_i, i = args
        s = jnp.einsum('bqhmd,bkhmd->bhmqk', q_i, kf) * (DB ** -0.5)
        qpos = i * Q_BLOCK + jnp.arange(Q_BLOCK)
        s = jnp.where(kpos[None, :] <= qpos[:, None], s, -jnp.inf)
        return jnp.einsum('bhqk,bkhe->bqhe', diff_weights(s, lam), vf)

    o = lax.map(block, (qb, jnp.arange(nb)))
    return jnp.moveaxis(o, 0, 1).reshape(bsz, t, H_B, 2 * DB)

def diff_attn_paged(q, k, v, lam, k_pool, v_pool, page_table):
    bsz, t = q.shape[:2]
    kp = k_pool[page_table].reshape(bsz, -1, H_B, 2, DB).astype(F32)
    vp = v_pool[page_table].reshape(bsz, -1, H_B, 2 * DB).astype(F32)
    past = kp.shape[1]
    qf = q.astype(F32)
    s_past = jnp.einsum('bqhmd,bkhmd->bhmqk', qf, kp)
    s_new = jnp.einsum('bqhmd,bkhmd->bhmqk', qf, k.astype(F32))
    s_new = jnp.where(jnp.tril(jnp.ones((t, t), bool)), s_new, -jnp.inf)
    s = jnp.concatenate([s_past, s_new], axis=-1) * (DB ** -0.5)
    wts = diff_weights(s, lam)
    return (jnp.einsum('bhqk,bkhe->bqhe', wts[..., :past], vp)
            + jnp.einsum('bhqk,bkhe->bqhe', wts[..., past:], v.astype(F32)))

def rwkv7_mixer(cols, prev, s0, mu, w0, w2, a0, a2, g2, k_k, k_a, r_k, lnx_w, lnx_b):
    bsz, t, _ = cols.shape
    shifted = jnp.concatenate([prev[:, None].astype(cols.dtype), cols[:, :-1]], axis=1)
    xs = cols + (shifted - cols) * mu
    r, k, v, wd, ad, gd = jnp.split(xs.astype(F32), [W_C, 2 * W_C, 3 * W_C, 3 * W_C + DECAY_LORA,
                                                     3 * W_C + DECAY_LORA + AAA_LORA], axis=-1)
    w = -jax.nn.softplus(-(w0 + jnp.tanh(wd) @ w2)) - 0.5
    decay = jnp.exp(-jnp.exp(w))
    a = jax.nn.sigmoid(a0 + ad @ a2)
    gate = jax.nn.sigmoid(gd) @ g2

    def heads(z):
        return z.reshape(bsz, t, H_C, HEAD_DIM)

    kk = heads(k * k_k)
    kk = kk * lax.rsqrt(jnp.sum(kk * kk, axis=-1, keepdims=True) + 1e-12)
    k = k * (1.0 + (a - 1.0) * k_a)
    r, k, v, decay, a = map(heads, (r, k, v, decay, a))

    def step(s, inp):
        r_t, k_t, v_t, d_t, kk_t, a_t = inp
        sa = jnp.einsum('bhvk,bhk->bhv', s, -kk_t)
        s = (s * d_t[:, :, None, :] + sa[..., None] * (kk_t * a_t)[:, :, None, :]
             + v_t[..., None] * k_t[:, :, None, :])
        return s, jnp.einsum('bhvk,bhk->bhv', s, r_t)

    seq = tuple(jnp.moveaxis(z, 1, 0) for z in (r, k, v, decay, kk, a))
    s, o = lax.scan(step, s0.astype(F32), seq)
    o = jnp.moveaxis(o, 0, 1)
    mean = jnp.mean(o, axis=-1, keepdims=True)
    var = jnp.mean(jnp.square(o - mean), axis=-1, keepdims=True)
    o = ((o - mean) * lax.rsqrt(var + RWKV_GN_EPS)).reshape(bsz, t, W_C) * lnx_w + lnx_b
    bonus = jnp.sum(r * k * r_k, axis=-1, keepdims=True) * v
    o = (o + bonus.reshape(bsz, t, W_C)) * gate
    return o.astype(cols.dtype), cols[:, -1], s.astype(cols.dtype)

def mem_project(mem, g, wk, wv):
    m = rmsnorm(mem, g)
    bsz = mem.shape[0]
    return ((m @ wk).reshape(bsz, -1, MEM_HEADS, MEM_HD), (m @ wv).reshape(bsz, -1, MEM_HEADS, MEM_HD))

def mem_attend(h, mem_k, mem_v, wq, wo):
    bsz, t, _ = h.shape
    q = (h @ wq).reshape(bsz, t, MEM_HEADS, MEM_HD)
    s = jnp.einsum('bthd,bmhd->bhtm', q.astype(F32), mem_k.astype(F32)) * (MEM_HD ** -0.5)
    p = jax.nn.softmax(s, axis=-1)
    o = jnp.einsum('bhtm,bmhd->bthd', p, mem_v.astype(F32)).reshape(bsz, t, MEM_INNER)
    return o.astype(h.dtype) @ wo

def conv_ffn(h, buf, w_in, conv_w, conv_b, w_out):
    gate, val = jnp.split(h @ w_in, 2, axis=-1)
    gate, new_buf = causal_dwconv(gate, buf, conv_w, conv_b)
    return (jax.nn.silu(gate) * val) @ w_out, new_buf

def trunk_layer(x, mem_k, mem_v, gdn_buf, gdn_s, rw_prev, rw_s, ffn_buf, attn_fn, lam_init, p):
    bsz, t, _ = x.shape
    h = rmsnorm(x, p['norm_mix'])
    cols = h @ p['w_in']
    a_cols, b_cols, c_cols = jnp.split(cols, [A_COLS, A_COLS + B_COLS], axis=-1)
    o_a, gdn_buf, gdn_s = gdn_mixer(a_cols, gdn_buf, gdn_s, p['gdn_conv_w'], p['gdn_a_log'],
                                    p['gdn_dt_bias'], p['gdn_norm'])
    q_b, k_b, v_b = jnp.split(b_cols, 3, axis=-1)
    q_b = q_b.reshape(bsz, t, H_B, 2, DB)
    k_b = k_b.reshape(bsz, t, H_B, 2, DB)
    v_b = v_b.reshape(bsz, t, H_B, 2 * DB)
    lam = diff_lambda(p['diff_lq1'], p['diff_lk1'], p['diff_lq2'], p['diff_lk2'], lam_init)
    o_b = attn_fn(q_b, k_b, v_b, lam)
    o_b = (rmsnorm(o_b, p['diff_subln']) * (1.0 - lam_init)).reshape(bsz, t, W_B).astype(x.dtype)
    o_c, rw_prev, rw_s = rwkv7_mixer(c_cols, rw_prev, rw_s, p['rw_mu'], p['rw_w0'], p['rw_w2'], p['rw_a0'],
                                     p['rw_a2'], p['rw_g2'], p['rw_k_k'], p['rw_k_a'], p['rw_r_k'],
                                     p['rw_lnx_w'], p['rw_lnx_b'])
    x = x + jnp.concatenate([o_a, o_b, o_c], axis=-1) @ p['w_out']
    x = x + mem_attend(rmsnorm(x, p['norm_mem']), mem_k, mem_v, p['mem_wq'], p['mem_wo'])
    f, ffn_buf = conv_ffn(rmsnorm(x, p['norm_ffn']), ffn_buf, p['ffn_w_in'], p['ffn_conv_w'],
                          p['ffn_conv_b'], p['ffn_w_out'])
    x = x + f
    return x, k_b.reshape(bsz, t, H_B, 2 * DB), v_b, gdn_buf, gdn_s, rw_prev, rw_s, ffn_buf

def setup_inputs(seed: int = 0) -> dict:
    key = jax.random.key(seed)
    ks = iter(jax.random.split(key, 64))

    def nrm(shape, scale=1.0):
        return jax.random.normal(next(ks), shape, F32) * scale

    def gain(shape, base=1.0):
        return base + 0.02 * jax.random.normal(next(ks), shape, F32)

    def unif(shape, lo, hi):
        return jax.random.uniform(next(ks), shape, F32, minval=lo, maxval=hi)

    n_pages = PAST_LEN // PAGE_SIZE
    n_used = DEC_BATCH * n_pages
    n_pool = n_used + n_used // 4
    page_table = jax.random.permutation(next(ks), n_pool)[:n_used].reshape(DEC_BATCH, n_pages).astype(jnp.int32)
    L = DEPTH
    return {
        'x_prompt': nrm((BATCH, SEQ, D_MODEL)),
        'x_sample': nrm((DEC_BATCH, DEC_SEQ, D_MODEL)),
        'cache_diff_k': nrm((L, n_pool, PAGE_SIZE, H_B, 2 * DB)),
        'cache_diff_v': nrm((L, n_pool, PAGE_SIZE, H_B, 2 * DB)),
        'state_gdn_conv': nrm((L, DEC_BATCH, GDN_CONV - 1, 3 * W_A)),
        'state_gdn': nrm((L, DEC_BATCH, H_A, HEAD_DIM, HEAD_DIM), 0.5),
        'state_rwkv_shift': nrm((L, DEC_BATCH, C_COLS)),
        'state_rwkv': nrm((L, DEC_BATCH, H_C, HEAD_DIM, HEAD_DIM), 0.5),
        'state_ffn_conv': nrm((L, DEC_BATCH, FFN_CONV - 1, D_FF)),
        'cache_mem_k': nrm((L, DEC_BATCH, MEM_TOKENS, MEM_HEADS, MEM_HD)),
        'cache_mem_v': nrm((L, DEC_BATCH, MEM_TOKENS, MEM_HEADS, MEM_HD)),
        'page_table': page_table,
        'mem_prompt': nrm((BATCH, MEM_TOKENS, D_MODEL)),
        'norm_mix': gain((L, D_MODEL)),
        'w_in': nrm((L, D_MODEL, N_IN_COLS), D_MODEL ** -0.5),
        'gdn_conv_w': nrm((L, GDN_CONV, 3 * W_A), GDN_CONV ** -0.5),
        'gdn_a_log': jnp.log(unif((L, H_A), 1.0, 16.0)),
        'gdn_dt_bias': nrm((L, H_A), 0.1),
        'gdn_norm': gain((L, HEAD_DIM)),
        'diff_lq1': nrm((L, DB), 0.1),
        'diff_lk1': nrm((L, DB), 0.1),
        'diff_lq2': nrm((L, DB), 0.1),
        'diff_lk2': nrm((L, DB), 0.1),
        'diff_subln': gain((L, 2 * DB)),
        'rw_mu': unif((L, C_COLS), 0.0, 1.0),
        'rw_w0': unif((L, W_C), -6.5, -1.5),
        'rw_w2': nrm((L, DECAY_LORA, W_C), 0.1 * DECAY_LORA ** -0.5),
        'rw_a0': nrm((L, W_C), 0.1),
        'rw_a2': nrm((L, AAA_LORA, W_C), AAA_LORA ** -0.5),
        'rw_g2': nrm((L, GATE_LORA, W_C), GATE_LORA ** -0.5),
        'rw_k_k': gain((L, W_C), 0.85),
        'rw_k_a': gain((L, W_C), 1.0),
        'rw_r_k': nrm((L, H_C, HEAD_DIM), 0.1),
        'rw_lnx_w': gain((L, W_C)),
        'rw_lnx_b': nrm((L, W_C), 0.02),
        'w_out': nrm((L, MIX_WIDTH, D_MODEL), MIX_WIDTH ** -0.5),
        'norm_mem': gain((L, D_MODEL)),
        'norm_mem_kv': gain((L, D_MODEL)),
        'mem_wq': nrm((L, D_MODEL, MEM_INNER), D_MODEL ** -0.5),
        'mem_wk': nrm((L, D_MODEL, MEM_INNER), D_MODEL ** -0.5),
        'mem_wv': nrm((L, D_MODEL, MEM_INNER), D_MODEL ** -0.5),
        'mem_wo': nrm((L, MEM_INNER, D_MODEL), MEM_INNER ** -0.5),
        'norm_ffn': gain((L, D_MODEL)),
        'ffn_w_in': nrm((L, D_MODEL, 2 * D_FF), D_MODEL ** -0.5),
        'ffn_conv_w': nrm((L, FFN_CONV, D_FF), FFN_CONV ** -0.5),
        'ffn_conv_b': nrm((L, D_FF), 0.02),
        'ffn_w_out': nrm((L, D_FF, D_MODEL), D_FF ** -0.5),
        'norm_final': gain((D_MODEL,)),
    }

def reference(x_prompt, x_sample, cache_diff_k, cache_diff_v, state_gdn_conv, state_gdn, state_rwkv_shift,
              state_rwkv, state_ffn_conv, cache_mem_k, cache_mem_v, page_table, mem_prompt, norm_mix, w_in,
              gdn_conv_w, gdn_a_log, gdn_dt_bias, gdn_norm, diff_lq1, diff_lk1, diff_lq2, diff_lk2, diff_subln,
              rw_mu, rw_w0, rw_w2, rw_a0, rw_a2, rw_g2, rw_k_k, rw_k_a, rw_r_k, rw_lnx_w, rw_lnx_b, w_out,
              norm_mem, norm_mem_kv, mem_wq, mem_wk, mem_wv, mem_wo, norm_ffn, ffn_w_in, ffn_conv_w, ffn_conv_b,
              ffn_w_out, norm_final):
    bp = x_prompt.shape[0]
    dt = x_prompt.dtype
    xp, xs = x_prompt, x_sample
    p_k, p_v, p_gc, p_gs, p_rp, p_rs, p_fc, p_mk, p_mv = [], [], [], [], [], [], [], [], []
    s_k, s_v, s_gc, s_gs, s_rp, s_rs, s_fc = [], [], [], [], [], [], []
    for l in range(DEPTH):
        lam_init = 0.8 - 0.6 * math.exp(-0.3 * l)
        p = dict(norm_mix=norm_mix[l], w_in=w_in[l], gdn_conv_w=gdn_conv_w[l], gdn_a_log=gdn_a_log[l],
                 gdn_dt_bias=gdn_dt_bias[l], gdn_norm=gdn_norm[l], diff_lq1=diff_lq1[l], diff_lk1=diff_lk1[l],
                 diff_lq2=diff_lq2[l], diff_lk2=diff_lk2[l], diff_subln=diff_subln[l], rw_mu=rw_mu[l],
                 rw_w0=rw_w0[l], rw_w2=rw_w2[l], rw_a0=rw_a0[l], rw_a2=rw_a2[l], rw_g2=rw_g2[l],
                 rw_k_k=rw_k_k[l], rw_k_a=rw_k_a[l], rw_r_k=rw_r_k[l], rw_lnx_w=rw_lnx_w[l],
                 rw_lnx_b=rw_lnx_b[l], w_out=w_out[l], norm_mem=norm_mem[l], mem_wq=mem_wq[l],
                 mem_wo=mem_wo[l], norm_ffn=norm_ffn[l], ffn_w_in=ffn_w_in[l], ffn_conv_w=ffn_conv_w[l],
                 ffn_conv_b=ffn_conv_b[l], ffn_w_out=ffn_w_out[l])
        mk, mv = mem_project(mem_prompt, norm_mem_kv[l], mem_wk[l], mem_wv[l])
        xp, k_new, v_new, gc, gs, rp, rs, fc = trunk_layer(
            xp, mk, mv,
            jnp.zeros((bp, GDN_CONV - 1, 3 * W_A), dt), jnp.zeros((bp, H_A, HEAD_DIM, HEAD_DIM), F32),
            jnp.zeros((bp, C_COLS), dt), jnp.zeros((bp, H_C, HEAD_DIM, HEAD_DIM), F32),
            jnp.zeros((bp, FFN_CONV - 1, D_FF), dt), diff_attn_prompt, lam_init, p)
        p_k.append(k_new); p_v.append(v_new); p_gc.append(gc); p_gs.append(gs)
        p_rp.append(rp); p_rs.append(rs); p_fc.append(fc); p_mk.append(mk); p_mv.append(mv)
        attn_s = functools.partial(diff_attn_paged, k_pool=cache_diff_k[l], v_pool=cache_diff_v[l],
                                   page_table=page_table)
        xs, k_new, v_new, gc, gs, rp, rs, fc = trunk_layer(
            xs, cache_mem_k[l], cache_mem_v[l], state_gdn_conv[l], state_gdn[l], state_rwkv_shift[l],
            state_rwkv[l], state_ffn_conv[l], attn_s, lam_init, p)
        s_k.append(k_new); s_v.append(v_new); s_gc.append(gc); s_gs.append(gs)
        s_rp.append(rp); s_rs.append(rs); s_fc.append(fc)
    y_prompt = rmsnorm(xp, norm_final)
    y_sample = rmsnorm(xs, norm_final)
    return (y_prompt, y_sample,
            jnp.stack(p_k), jnp.stack(p_v), jnp.stack(p_gc), jnp.stack(p_gs), jnp.stack(p_rp),
            jnp.stack(p_rs), jnp.stack(p_fc), jnp.stack(p_mk), jnp.stack(p_mv),
            jnp.stack(s_k), jnp.stack(s_v), jnp.stack(s_gc), jnp.stack(s_gs), jnp.stack(s_rp),
            jnp.stack(s_rs), jnp.stack(s_fc))


_drawn_inputs = setup_inputs


def setup_inputs(seed=0):
    import zlib

    import numpy as np

    out = dict(_drawn_inputs(seed))
    spreads = {}
    factors = {'gdn_dt_bias': 8.0,
     'gdn_norm': 8.0,
     'diff_lq1': 8.0,
     'diff_lk1': 7.261,
     'diff_lq2': 8.0,
     'diff_subln': 7.963,
     'rw_w2': 8.0,
     'rw_lnx_w': 8.0,
     'rw_lnx_b': 8.0,
     'norm_mem': 8.0,
     'norm_mem_kv': 2.721,
     'norm_ffn': 7.478,
     'ffn_conv_b': 17.26,
     'norm_final': 24.469}
    for name, (base, spread) in spreads.items():
        noise = np.random.default_rng([zlib.crc32(name.encode()), seed]).standard_normal(out[name].shape)
        drawn = base * np.exp(spread * noise) if base else spread * noise
        out[name] = __import__('jax').numpy.asarray(drawn.astype(out[name].dtype))
    for name, factor in factors.items():
        out[name] = (out[name] * factor).astype(out[name].dtype)
    return out
```

```python
import math
from contextlib import ExitStack

import numpy as np

import concourse.bass as bass
from concourse import mybir

F32 = mybir.dt.float32
I32 = mybir.dt.int32
ACT = mybir.ActivationFunctionType
ALU = mybir.AluOpType
AX = mybir.AxisListType

P = 128
D = 1024
KD = D // P
SEQ = 2048
NB, NQ = 8, 4
NS = NB * NQ
TOK = SEQ + NS
TILES = SEQ // P
HD = 64
W_A, W_B, W_C = 384, 256, 384
H_A, H_B, H_C = 6, 4, 6
DB = 32
A_COLS, B_COLS, C_COLS = 4 * W_A + 2 * H_A, 3 * W_B, 3 * W_C + 256
N_IN = A_COLS + B_COLS + C_COLS
D_FF = 2816
FB = D_FF // P
MEM, MH, MHD = 256, 4, 128
MI = MH * MHD
PAGES, PAGE = 64, 128
CH = 416
NCH = TOK // CH
LASTP = SEQ - (NCH - 1) * CH
EPS = 1e-6
LAM_INIT = 0.8 - 0.6 * math.exp(-0.3 * 0)
NEG = -1.0e30

B_QKV, B_Z, B_DIFF, B_RWKV, B_BETA = 0, 9, 12, 18, 29
N_BLOCKS = 30


class Steps:

    def __init__(self, sem, names):
        self.sem, self.names = sem, names.split()

    def at(self, name, t=0):
        return t * len(self.names) + (self.names.index(name) + 1)


def sweep(eng, n, body):
    for t in range(min(n, 2)):
        body(t, t)
    pairs = (n - 2) // 2
    if pairs > 1:
        with eng.Fori(0, pairs) as i:
            for u in range(2):
                body(2 * i + (2 + u), u)
    elif pairs == 1:
        for t in (2, 3):
            body(t, t % 2)
    if n > 2 and n % 2:
        body(n - 1, (n - 1) % 2)


def early(t, back=2):
    return isinstance(t, int) and t < back


def bc(ap, n):
    return ap.unsqueeze(len(ap.shape)).to_broadcast(list(ap.shape) + [n])


def mid(ap, n):
    return ap.unsqueeze(1).to_broadcast([ap.shape[0], n, ap.shape[1]])


class Prog:

    def __init__(self, nc, ins, outs):
        self.nc, self.i, self.o = nc, ins, outs
        self.n = 0

    def open(self):
        return Stage(self.nc)


class Stage:

    count = 0

    def __init__(self, nc):
        self.nc, self.ctx, self.sems = nc, ExitStack(), []

    def __enter__(self):
        Stage.count += 1
        self.tag = f"s{Stage.count}_"
        return self

    def __exit__(self, *a):
        if self.sems and not any(a):
            with self.nc.Block() as block:
                @block.sync
                def _(sp):
                    for s in self.sems:
                        sp.sem_clear(s)
        return self.ctx.__exit__(*a)

    def sb(self, name, shape, dt=F32):
        return self.ctx.enter_context(self.nc.sbuf_tensor(self.tag + name, shape, dt))

    def ps(self, name, shape, dt=F32):
        return self.ctx.enter_context(self.nc.psum_tensor(self.tag + name, shape, dt))

    def sem(self, name):
        self.sems.append(self.ctx.enter_context(self.nc.semaphore(self.tag + name)))
        return self.sems[-1]

    def steps(self, name, names):
        return Steps(self.sem(name), names)


def rows(ap, t, n=P):
    return ap[bass.ds(t * P, n), :]


def load_constants(nc, pr):
    i = pr.i
    with Stage(nc) as st:
        s = st.sem("const_in")
        n = 0
        with nc.Block() as block:
            @block.sync
            def _(sp):
                n = 0
                with nc.allow_non_contiguous_dma("small vectors to columns"):
                    for dst, src in pr.const_loads:
                        sp.dma_start(dst, src).then_inc(s, 16)
                        n += 16
                sp.wait_ge(s, n)


def norm_transpose(nc, pr, sources, g_cols, hT, n_tiles=TILES, tail=NS):
    with Stage(nc) as st:
        x = st.sb("x", [P, 2, D])
        xn = st.sb("xn", [P, 2, D])
        sq = st.sb("sq", [P, D])
        ss = st.sb("ss", [P, 2])
        tp = [[st.ps(f"tp{u}{c}", [P, 4, P]) for c in range(2)] for u in range(2)]
        x_in = [st.sem(f"x_in{u}") for u in range(2)]
        A = st.steps("act_steps", "square log rstd scaled")
        T = st.steps("pe_steps", "t0 t1")
        V = st.steps("dve_steps", "h0 h1")

        def item(eng, body):
            if n_tiles > 1:
                sweep(eng, n_tiles, lambda t, u: body(t, u, P))
            if tail:
                body(n_tiles, n_tiles % 2, tail)

        with nc.Block() as block:
            @block.sync
            def _(sp):
                def body(t, u, n):
                    if not early(t):
                        sp.wait_ge(A.sem, A.at("scaled", t - 2))
                    sp.dma_start(x[0:n, u, :], sources(t, n)).then_inc(x_in[u], 16)
                item(sp, body)

            @block.scalar
            def _(act):
                def body(t, u, n):
                    act.wait_ge(x_in[u], (t - u) * 8 + 16)
                    act.activation(sq[0:n, :], x[0:n, u, :], ACT.Square, accum_out=ss[0:n, u:u + 1])\
                       .then_inc(A.sem, 1)
                    act.wait_ge(A.sem, A.at("square", t))
                    act.activation(ss[0:n, u:u + 1], ss[0:n, u:u + 1], ACT.Ln, scale=1.0 / D, bias=pr.eps[0:n, :])\
                       .then_inc(A.sem, 1)
                    act.wait_ge(A.sem, A.at("log", t))
                    act.activation(ss[0:n, u:u + 1], ss[0:n, u:u + 1], ACT.Exp, scale=-0.5).then_inc(A.sem, 1)
                    act.wait_ge(A.sem, A.at("rstd", t))
                    if not early(t):
                        act.wait_ge(T.sem, T.at("t1", t - 2))
                    act.activation(xn[0:n, u, :], x[0:n, u, :], ACT.Copy, scale=ss[0:n, u:u + 1])\
                       .then_inc(A.sem, 1)
                item(act, body)

            @block.tensor
            def _(pe):
                def body(t, u, n):
                    pe.wait_ge(A.sem, A.at("scaled", t))
                    for c in range(2):
                        if not early(t):
                            pe.wait_ge(V.sem, V.at(f"h{c}", t - 2))
                        for k in range(4):
                            kk = 4 * c + k
                            mm = pe.transpose(tp[u][c][:, k, 0:n], xn[0:n, u, kk * P:(kk + 1) * P],
                                              pr.ident[0:n, 0:n])
                        mm.then_inc(T.sem, 1)
                item(pe, body)

            @block.vector
            def _(dve):
                def body(t, u, n):
                    for c in range(2):
                        dve.wait_ge(T.sem, T.at(f"t{c}", t))
                        dve.tensor_tensor(hT[:, 4 * c:4 * c + 4, bass.ds(t * P, n)], tp[u][c][:, :, 0:n],
                                          bc(g_cols[:, 4 * c:4 * c + 4], n), ALU.mult).then_inc(V.sem, 1)
                item(dve, body)


def project(nc, pr, hT, n_blocks, col0, row0, kind, m=P, halo=0, taps=None, state_in=None, saved=None):
    w = pr.i["w_in"][0].rearrange("(k p) n -> p k n", p=P)
    plain = kind in ("plain", "silu")
    with Stage(nc) as st:
        W = st.sb("W", [P, 2, KD, m])
        raw_p = st.sb("raw_p", [P, 2, halo + SEQ]) if halo else None
        raw_s = st.sb("raw_s", [P, 2, NB, halo + NQ]) if halo else None
        mix = st.sb("mix", [P, TOK]) if kind in ("shift", "conv") else None
        out = st.sb("out", [P, 2, TOK])
        acc = [st.ps(f"acc{c}", [P, 512]) for c in range(NCH)]
        w_in = [st.sem(f"w_in{u}") for u in range(2)]
        stored = [st.sem(f"stored{u}") for u in range(2)]
        cleared = st.sem("halo_cleared")
        T = st.steps("pe_steps", " ".join(f"c{c}" for c in range(NCH)))
        evacs = " ".join(f"e{c}" for c in range(NCH))
        A = st.steps("act_steps", evacs + {"plain": "", "silu": "", "conv": " halo final", "shift": " halo"}[kind])
        V = st.steps("dve_steps", "a b c d saved")
        with nc.Block() as block:
            @block.sync
            def _(sp):
                def body(t, u):
                    if not early(t):
                        sp.wait_ge(T.sem, T.at(f"c{NCH - 1}", t - 2))
                    sp.dma_start(W[:, u, :, :], w[:, :, bass.ds(t * P + col0, m)]).then_inc(w_in[u], 16)
                sweep(sp, n_blocks, body)

            @block.tensor
            def _(pe):
                def body(t, u):
                    pe.wait_ge(w_in[u], (t - u) * 8 + 16)
                    for c in range(NCH):
                        if not early(t, 1):
                            pe.wait_ge(A.sem, A.at(f"e{c}", t - 1))
                        for k in range(KD):
                            mm = pe.matmul(acc[c][0:m, 0:CH], W[:, u, k, :], hT[:, k, c * CH:(c + 1) * CH],
                                           start=(k == 0), stop=(k == KD - 1))
                        mm.then_inc(T.sem, 1)
                sweep(pe, n_blocks, body)

            @block.scalar
            def _(act):
                def store(t, u):
                    act.dma_start(pr.cols[bass.ds(t + row0, 1), 0:m, :].rearrange("a p n -> p (a n)"),
                                  out[0:m, u, :]).then_inc(stored[u], 16)

                def body(t, u):
                    if not early(t):
                        if plain:
                            act.wait_ge(stored[u], (t - u) * 8)
                        else:
                            act.wait_ge(V.sem, V.at("saved", t - 2))
                    for c in range(NCH):
                        act.wait_ge(T.sem, T.at(f"c{c}", t))
                        n = CH if c < NCH - 1 else LASTP
                        if plain:
                            act.activation(out[0:m, u, c * CH:(c + 1) * CH], acc[c][0:m, 0:CH],
                                           ACT.Silu if kind == "silu" else ACT.Copy).then_inc(A.sem, 1)
                            continue
                        last = act.activation(raw_p[:, u, halo + c * CH:halo + c * CH + n], acc[c][:, 0:n], ACT.Copy)
                        if c == NCH - 1:
                            last = act.activation(raw_s[:, u, :, halo:halo + NQ],
                                                  acc[c][:, n:CH].rearrange("p (b q) -> p b q", q=NQ), ACT.Copy)
                        last.then_inc(A.sem, 1)
                    if plain:
                        act.wait_ge(A.sem, A.at(f"e{NCH - 1}", t))
                        store(t, u)
                        return
                    act.activation(raw_s[:, u, :, 0:halo], state_in[:, bass.ds(t, 1), :].rearrange(
                        "p a (b j) -> p (a b) j", j=halo), ACT.Copy).then_inc(A.sem, 1)
                    act.wait_ge(V.sem, V.at("d", t))
                    if kind == "conv":
                        if not early(t):
                            act.wait_ge(stored[u], (t - u) * 8)
                        act.activation(out[:, u, :], mix[:, :], ACT.Silu).then_inc(A.sem, 1)
                        act.wait_ge(A.sem, A.at("final", t))
                    store(t, u)
                sweep(act, n_blocks, body)
                for u in range(min(2, n_blocks)):
                    act.wait_ge(stored[u], 16 * ((n_blocks - u + 1) // 2))

            @block.vector
            def _(dve):
                if plain:
                    return
                dve.memset(raw_p[:, :, 0:halo], 0.0).then_inc(cleared, 1)
                dve.wait_ge(cleared, 1)

                def body(t, u):
                    dve.wait_ge(A.sem, A.at("halo", t))
                    op, os = out[:, u, 0:SEQ], out[:, u, SEQ:TOK].rearrange("p (b q) -> p b q", q=NQ)
                    mp, ms = mix[:, 0:SEQ], mix[:, SEQ:TOK].rearrange("p (b q) -> p b q", q=NQ)
                    if kind == "conv":
                        if not early(t, 1):
                            dve.wait_ge(A.sem, A.at("final", t - 1))
                        for j in range(4):
                            tap = taps[:, bass.ds(t, 1), j:j + 1].rearrange("p a b -> p (a b)")
                            rp, rs = raw_p[:, u, j:j + SEQ], raw_s[:, u, :, j:j + NQ]
                            if j == 0:
                                dve.tensor_scalar(ms, rs, tap, None, ALU.mult)
                                dve.tensor_scalar(mp, rp, tap, None, ALU.mult).then_inc(V.sem, 1)
                            else:
                                dve.wait_ge(V.sem, V.at("abcd"[j - 1], t))
                                dve.scalar_tensor_tensor(ms, rs, tap, ms, ALU.mult, ALU.add)
                                dve.scalar_tensor_tensor(mp, rp, tap, mp, ALU.mult, ALU.add).then_inc(V.sem, 1)
                    else:
                        mu = taps[:, bass.ds(t, 1), 0:1].rearrange("p a b -> p (a b)")
                        if not early(t, 1):
                            dve.wait_ge(V.sem, V.at("d", t - 1))
                        if not early(t):
                            dve.wait_ge(stored[u], (t - u) * 8)
                        dve.tensor_tensor(mp, raw_p[:, u, 0:SEQ], raw_p[:, u, 1:SEQ + 1], ALU.subtract)\
                           .then_inc(V.sem, 1)
                        dve.tensor_tensor(ms, raw_s[:, u, :, 0:NQ], raw_s[:, u, :, 1:NQ + 1], ALU.subtract)\
                           .then_inc(V.sem, 1)
                        dve.wait_ge(V.sem, V.at("b", t))
                        dve.scalar_tensor_tensor(op, mp, mu, raw_p[:, u, 1:SEQ + 1], ALU.mult, ALU.add)\
                           .then_inc(V.sem, 1)
                        dve.scalar_tensor_tensor(os, ms, mu, raw_s[:, u, :, 1:NQ + 1], ALU.mult, ALU.add)\
                           .then_inc(V.sem, 1)
                    dve.tensor_copy(saved[:, bass.ds(t, 1), 0:halo], raw_p[:, u, SEQ:SEQ + halo].unsqueeze(1))
                    dve.tensor_copy(saved[:, bass.ds(t, 1), halo:halo * (NB + 1)].rearrange(
                        "p a (b j) -> p (a b) j", j=halo), raw_s[:, u, :, NQ:NQ + halo]).then_inc(V.sem, 1)
                sweep(dve, n_blocks, body)


def flip_blocks(nc, pr, jobs):
    with Stage(nc) as st:
        tp = [st.ps(f"tp{u}", [P, P]) for u in range(4)]
        done, copied = st.sem("transposed"), st.sem("copied")
        with nc.Block() as block:
            @block.tensor
            def _(pe):
                for j, (src, dst) in enumerate(jobs):
                    if j >= 4:
                        pe.wait_ge(copied, j - 3)
                    n, m = src.shape
                    pe.transpose(tp[j % 4][0:m, 0:n], src, pr.ident[0:n, 0:n]).then_inc(done, 1)

            @block.vector
            def _(dve):
                for j, (src, dst) in enumerate(jobs):
                    n, m = src.shape
                    dve.wait_ge(done, j + 1)
                    dve.tensor_copy(dst, tp[j % 4][0:m, 0:n]).then_inc(copied, 1)


def copy_in(nc, pairs):
    with Stage(nc) as st:
        s = st.sem("arrived")
        with nc.Block() as block:
            @block.sync
            def _(sp):
                with nc.allow_non_contiguous_dma("small vectors to columns"):
                    for dst, src in pairs:
                        sp.dma_start(dst, src).then_inc(s, 16)
                sp.wait_ge(s, 16 * len(pairs))


def lagged(eng, parts):
    def step(t, u):
        for j, part in enumerate(parts):
            if early(t, j):
                break
            part(t - j, (u + j) % 2, P)
    sweep(eng, TILES, step)
    for t in range(TILES, TILES + len(parts)):
        for j, part in enumerate(parts):
            if t - j <= TILES:
                part(t - j, (t - j) % 2, P if t - j < TILES else NS)


def norm_act(act, A, ready, x, sq, ss, xn, t, n, eps, xn_free):
    ready()
    if not early(t, 1):
        act.wait_ge(A.sem, A.at("scaled", t - 1))
    act.activation(sq[0:n, :], x, ACT.Square, accum_out=ss[0:n, :]).then_inc(A.sem, 1)
    act.wait_ge(A.sem, A.at("square", t))
    act.activation(ss[0:n, :], ss[0:n, :], ACT.Ln, scale=1.0 / D, bias=eps[0:n, :]).then_inc(A.sem, 1)
    act.wait_ge(A.sem, A.at("log", t))
    act.activation(ss[0:n, :], ss[0:n, :], ACT.Exp, scale=-0.5).then_inc(A.sem, 1)
    act.wait_ge(A.sem, A.at("rstd", t))
    xn_free()
    act.activation(xn, x, ACT.Copy, scale=ss[0:n, :]).then_inc(A.sem, 1)


def mix_out(nc, pr, x_rows, g_mem, hT, subln):
    with Stage(nc) as st:
        w = st.sb("w_out", [P, KD, D])
        o = st.sb("o", [P, 2, D])
        x = st.sb("x", [P, 2, D])
        oT = st.sb("oT", [P, KD, P])
        sqb = st.sb("sqb", [P, W_B])
        ssb = st.sb("ssb", [P, H_B])
        x1 = st.sb("x1", [P, 2, D])
        sq = st.sb("sq", [P, D])
        ss = st.sb("ss", [P, 1])
        xn = st.sb("xn", [P, D])
        tp = [st.ps(f"tp{c}", [P, 4, P]) for c in range(2)]
        y = [st.ps(f"y{c}", [P, 512]) for c in range(2)]
        np_ = [st.ps(f"np{c}", [P, 4, P]) for c in range(2)]
        w_in = st.sem("w_in")
        loaded = [st.sem(f"loaded{u}") for u in range(2)]
        stored = [st.sem(f"stored{u}") for u in range(2)]
        T1, T2 = st.steps("pe_out", "o0 o1 m0 m1"), st.steps("pe_norm", "n0 n1")
        V1 = st.steps("dve_subln", "sqb sumb normb gainb")
        V2 = st.steps("dve_resid", "r0 r1 h0 h1")
        A1 = st.steps("act_subln", "logb rstdb oT0 oT1")
        A2 = st.steps("act_norm", "square log rstd scaled")
        ob = lambda u, n: o[0:n, u, W_A:W_A + W_B]
        heads = lambda ap: ap.rearrange("p (h d) -> p h d", d=HD)
        with nc.Block() as block:
            @block.sync
            def _(sp):
                sp.dma_start(w[:, :, :], pr.i["w_out"][0].rearrange("(k p) n -> p k n", p=P)).then_inc(w_in, 16)

                def load(t, u, n):
                    if not early(t):
                        sp.wait_ge(T1.sem, T1.at("o1", t - 2))
                        sp.wait_ge(V2.sem, V2.at("r1", t - 2))
                    sp.dma_start(o[0:n, u, :], rows(pr.o_raw, t, n)).then_inc(loaded[u], 16)
                    sp.dma_start(x[0:n, u, :], x_rows(t, n)).then_inc(loaded[u], 16)

                def store(t, u, n):
                    sp.wait_ge(V2.sem, V2.at("r1", t))
                    sp.dma_start(rows(pr.x1, t, n), x1[0:n, u, :]).then_inc(stored[u], 16)
                lagged(sp, [load, store])
                sp.wait_ge(stored[0], 16 * 9)
                sp.wait_ge(stored[1], 16 * 8)

            @block.tensor
            def _(pe):
                def out(t, u, n):
                    pe.wait_ge(V1.sem, V1.at("gainb", t))
                    for c in range(2):
                        if not early(t, 1):
                            pe.wait_ge(A1.sem, A1.at(f"oT{c}", t - 1))
                        for k in range(4):
                            mm = pe.transpose(tp[c][:, k, 0:n], o[0:n, u, (4 * c + k) * P:(4 * c + k + 1) * P],
                                              pr.ident[0:n, 0:n])
                        mm.then_inc(T1.sem, 1)
                    if isinstance(t, int) and t == 0:
                        pe.wait_ge(w_in, 16)
                    pe.wait_ge(A1.sem, A1.at("oT1", t))
                    for c in range(2):
                        if not early(t, 1):
                            pe.wait_ge(V2.sem, V2.at(f"r{c}", t - 1))
                        for k in range(KD):
                            mm = pe.matmul(y[c][0:n, :], oT[:, k, 0:n], w[:, k, c * 512:(c + 1) * 512],
                                           start=(k == 0), stop=(k == KD - 1))
                        mm.then_inc(T1.sem, 1)

                def norm(t, u, n):
                    pe.wait_ge(A2.sem, A2.at("scaled", t))
                    for c in range(2):
                        if not early(t, 1):
                            pe.wait_ge(V2.sem, V2.at(f"h{c}", t - 1))
                        for k in range(4):
                            mm = pe.transpose(np_[c][:, k, 0:n], xn[0:n, (4 * c + k) * P:(4 * c + k + 1) * P],
                                              pr.ident[0:n, 0:n])
                        mm.then_inc(T2.sem, 1)
                lagged(pe, [out, norm])

            @block.vector
            def _(dve):
                def sub(t, u, n):
                    dve.wait_ge(loaded[u], (t - u) * 16 + 32)
                    if not early(t, 1):
                        dve.wait_ge(V1.sem, V1.at("gainb", t - 1))
                    dve.tensor_tensor(sqb[0:n, :], ob(u, n), ob(u, n), ALU.mult).then_inc(V1.sem, 1)
                    dve.wait_ge(V1.sem, V1.at("sqb", t))
                    dve.tensor_reduce(ssb[0:n, :], heads(sqb[0:n, :]), AX.X, ALU.add).then_inc(V1.sem, 1)
                    dve.wait_ge(A1.sem, A1.at("rstdb", t))
                    dve.tensor_tensor(heads(ob(u, n)), heads(ob(u, n)), bc(ssb[0:n, :], HD), ALU.mult)\
                       .then_inc(V1.sem, 1)
                    dve.wait_ge(V1.sem, V1.at("normb", t))
                    dve.scalar_tensor_tensor(heads(ob(u, n)), heads(ob(u, n)), 1.0 - LAM_INIT, mid(subln[0:n, :], H_B),
                                             ALU.mult, ALU.mult).then_inc(V1.sem, 1)

                def resid(t, u, n):
                    if not early(t):
                        dve.wait_ge(stored[u], (t - u) * 8)
                        dve.wait_ge(A2.sem, A2.at("scaled", t - 2))
                    for c in range(2):
                        dve.wait_ge(T1.sem, T1.at(f"m{c}", t))
                        dve.tensor_tensor(x1[0:n, u, c * 512:(c + 1) * 512], y[c][0:n, :],
                                          x[0:n, u, c * 512:(c + 1) * 512], ALU.add).then_inc(V2.sem, 1)
                    for c in range(2):
                        dve.wait_ge(T2.sem, T2.at(f"n{c}", t))
                        dve.tensor_tensor(hT[:, 4 * c:4 * c + 4, bass.ds(t * P, n)], np_[c][:, :, 0:n],
                                          bc(g_mem[:, 4 * c:4 * c + 4], n), ALU.mult).then_inc(V2.sem, 1)
                lagged(dve, [sub, resid])

            @block.scalar
            def _(act):
                def sub(t, u, n):
                    act.wait_ge(V1.sem, V1.at("sumb", t))
                    act.activation(ssb[0:n, :], ssb[0:n, :], ACT.Ln, scale=1.0 / HD, bias=pr.eps[0:n, :])\
                       .then_inc(A1.sem, 1)
                    act.wait_ge(A1.sem, A1.at("logb", t))
                    act.activation(ssb[0:n, :], ssb[0:n, :], ACT.Exp, scale=-0.5).then_inc(A1.sem, 1)
                    if not early(t, 1):
                        act.wait_ge(T1.sem, T1.at("m1", t - 1))
                    for c in range(2):
                        act.wait_ge(T1.sem, T1.at(f"o{c}", t))
                        act.activation(oT[:, 4 * c:4 * c + 4, 0:n], tp[c][:, :, 0:n], ACT.Copy).then_inc(A1.sem, 1)

                def norm(t, u, n):
                    def free():
                        if not early(t, 1):
                            act.wait_ge(T2.sem, T2.at("n1", t - 1))
                    norm_act(act, A2, lambda: act.wait_ge(V2.sem, V2.at("r1", t)), x1[0:n, u, :], sq, ss,
                             xn[0:n, :], t, n, pr.eps, free)
                lagged(act, [sub, norm])


def mem_project(nc, pr, mT, mK_T, mV, out_k, out_v):
    with Stage(nc) as st:
        wk = st.sb("wk", [P, KD, MI])
        wv = st.sb("wv", [P, KD, MI])
        kr = st.sb("k_rows", [P, 2, MI])
        acc = [st.ps(f"acc{j}", [P, 512]) for j in range(8)]
        w_in, done, copied, stored = (st.sem(n) for n in ("w_in", "products", "copied", "stored"))
        view = lambda ap: ap.rearrange("a b h d -> (a b) (h d)") if len(ap.shape) == 4 else ap
        with nc.Block() as block:
            @block.sync
            def _(sp):
                for w, name in ((wk, "mem_wk"), (wv, "mem_wv")):
                    sp.dma_start(w[:, :, :], pr.i[name][0].rearrange("(k p) n -> p k n", p=P)).then_inc(w_in, 16)
                sp.wait_ge(copied, 8)
                sp.dma_start(out_k.rearrange("(c p) n -> p c n", p=P), kr[:, :, :]).then_inc(stored, 16)
                sp.dma_start(out_v.rearrange("(c p) n -> p c n", p=P), mV[:, :, :]).then_inc(stored, 16)
                sp.wait_ge(stored, 32)

            @block.tensor
            def _(pe):
                pe.wait_ge(w_in, 32)
                for j in range(8):
                    for k in range(KD):
                        if j < 4:
                            w = (wk, wv)[j // 2]
                            mm = pe.matmul(acc[j][:, :], mT[:, k, (j % 2) * P:(j % 2 + 1) * P], w[:, k, :],
                                           start=(k == 0), stop=(k == KD - 1))
                        else:
                            h = j - 4
                            mm = pe.matmul(acc[j][:, 0:MEM], wk[:, k, h * MHD:(h + 1) * MHD], mT[:, k, 0:MEM],
                                           start=(k == 0), stop=(k == KD - 1))
                    mm.then_inc(done, 1)

            @block.vector
            def _(dve):
                for j in range(8):
                    dve.wait_ge(done, j + 1)
                    dst = kr[:, j, :] if j < 2 else mV[:, j - 2, :] if j < 4 else mK_T[:, j - 4, :]
                    dve.tensor_copy(dst, acc[j][:, 0:dst.shape[1]]).then_inc(copied, 1)


def mem_attention(nc, pr, hT, g_ffn, mK_T, mV, sample_o):
    with Stage(nc) as st:
        wq = st.sb("wq", [P, KD, MI])
        wo = st.sb("wo", [P, MH, D])
        qT = st.sb("qT", [P, MH, P])
        prob = st.sb("prob", [P, 2, MH, MEM])
        top = st.sb("top", [P, 2, MH])
        den = st.sb("den", [P, 2, MH])
        pT = st.sb("pT", [P, 2, MH, P])
        oT = st.sb("oT", [P, MH, P])
        x1 = st.sb("x1", [P, 2, D])
        x2 = st.sb("x2", [P, 2, D])
        sq = st.sb("sq", [P, D])
        ss = st.sb("ss", [P, 1])
        xn = st.sb("xn", [P, D])
        q_ps = st.ps("q_ps", [P, MH, P])
        s_ps = [st.ps(f"s_ps{c}", [P, 2, MEM]) for c in range(2)]
        tp = [st.ps(f"tp{c}", [P, 4, P]) for c in range(2)]
        o_ps = st.ps("o_ps", [P, MH, P])
        y = [st.ps(f"y{c}", [P, 512]) for c in range(2)]
        w_in = st.sem("w_in")
        loaded = [st.sem(f"loaded{u}") for u in range(2)]
        stored = [st.sem(f"stored{u}") for u in range(2)]
        T1, T2, T3 = st.steps("pe_score", "q s0 s1"), st.steps("pe_apply", "p0 p1 o y0 y1"), st.steps("pe_norm", "n0 n1")
        A1, A2, A3 = st.steps("act_score", "q exp"), st.steps("act_apply", "p0 p1"), \
            st.steps("act_norm", "square log rstd scaled")
        V1, V2, V3 = st.steps("dve_top", "top neg"), st.steps("dve_apply", "inv norm o r0 r1"), \
            st.steps("dve_flip", "h0 h1")
        scale = float(MHD) ** -0.5
        with nc.Block() as block:
            @block.sync
            def _(sp):
                sp.dma_start(wq[:, :, :], pr.i["mem_wq"][0].rearrange("(k p) n -> p k n", p=P)).then_inc(w_in, 16)
                sp.dma_start(wo[:, :, :], pr.i["mem_wo"][0].rearrange("(k p) n -> p k n", p=P)).then_inc(w_in, 16)

                def load(t, u, n):
                    if not early(t):
                        sp.wait_ge(V2.sem, V2.at("r1", t - 2))
                    sp.dma_start(x1[0:n, u, :], rows(pr.x1, t, n)).then_inc(loaded[u], 16)

                def store(t, u, n):
                    sp.wait_ge(V2.sem, V2.at("r1", t))
                    sp.dma_start(rows(pr.x2, t, n), x2[0:n, u, :]).then_inc(stored[u], 16)
                lagged(sp, [load, store])
                sp.wait_ge(stored[0], 16 * 9)
                sp.wait_ge(stored[1], 16 * 8)

            @block.tensor
            def _(pe):
                def score(t, u, n):
                    if isinstance(t, int) and t == 0:
                        pe.wait_ge(w_in, 32)
                    if n == NS:
                        return
                    if not early(t, 1):
                        pe.wait_ge(A1.sem, A1.at("q", t - 1))
                    for h in range(MH):
                        for k in range(KD):
                            mm = pe.matmul(q_ps[:, h, :], wq[:, k, h * P:(h + 1) * P], hT[:, k, bass.ds(t * P, P)],
                                           start=(k == 0), stop=(k == KD - 1))
                    mm.then_inc(T1.sem, 1)
                    pe.wait_ge(A1.sem, A1.at("q", t))
                    for h in range(MH):
                        mm = pe.matmul(s_ps[h // 2][:, h % 2, :], qT[:, h, :], mK_T[:, h, :], start=True, stop=True)
                        if h % 2:
                            mm.then_inc(T1.sem, 1)

                def apply(t, u, n):
                    if n == P:
                        pe.wait_ge(V2.sem, V2.at("norm", t))
                        if not early(t, 2):
                            pe.wait_ge(V3.sem, V3.at("h1", t - 2))
                        for c in range(2):
                            for h in range(MH):
                                mm = pe.transpose(tp[c][:, h, :], prob[:, u, h, c * P:(c + 1) * P], pr.ident[:, :])
                            mm.then_inc(T2.sem, 1)
                        pe.wait_ge(A2.sem, A2.at("p1", t))
                        if not early(t, 1):
                            pe.wait_ge(V2.sem, V2.at("o", t - 1))
                        for h in range(MH):
                            for c in range(2):
                                mm = pe.matmul(o_ps[:, h, :], mV[:, c, h * P:(h + 1) * P], pT[:, c, h, :],
                                               start=(c == 0), stop=(c == 1))
                        mm.then_inc(T2.sem, 1)
                        pe.wait_ge(V2.sem, V2.at("o", t))
                    if not early(t, 1):
                        pe.wait_ge(V2.sem, V2.at("r1", t - 1))
                    for c in range(2):
                        for h in range(MH):
                            o = oT[:, h, :] if n == P else sample_o[:, h, :]
                            mm = pe.matmul(y[c][0:n, :], o, wo[:, h, c * 512:(c + 1) * 512],
                                           start=(h == 0), stop=(h == MH - 1))
                        mm.then_inc(T2.sem, 1)

                def norm(t, u, n):
                    pe.wait_ge(A3.sem, A3.at("scaled", t))
                    if t_plus_one(t):
                        pe.wait_ge(A2.sem, A2.at("p1", t + 1))
                    if not early(t, 1):
                        pe.wait_ge(V3.sem, V3.at("h1", t - 1))
                    for c in range(2):
                        for k in range(4):
                            mm = pe.transpose(tp[c][:, k, 0:n], xn[0:n, (4 * c + k) * P:(4 * c + k + 1) * P],
                                              pr.ident[0:n, 0:n])
                        mm.then_inc(T3.sem, 1)
                t_plus_one = lambda t: not (isinstance(t, int) and t + 1 >= TILES)
                lagged(pe, [score, apply, norm])

            @block.scalar
            def _(act):
                def score(t, u, n):
                    if n == NS:
                        return
                    act.wait_ge(T1.sem, T1.at("q", t))
                    if not early(t, 1):
                        act.wait_ge(T1.sem, T1.at("s1", t - 1))
                    act.activation(qT[:, :, :], q_ps[:, :, :], ACT.Copy, scale=scale).then_inc(A1.sem, 1)
                    act.wait_ge(V1.sem, V1.at("neg", t))
                    if not early(t):
                        act.wait_ge(T2.sem, T2.at("p1", t - 2))
                    for h in range(MH):
                        last = act.activation(prob[:, u, h, :], s_ps[h // 2][:, h % 2, :], ACT.Exp,
                                              bias=top[:, u, h:h + 1], accum_out=den[:, u, h:h + 1])
                    last.then_inc(A1.sem, 1)

                def apply(t, u, n):
                    if n == NS:
                        return
                    if not early(t, 1):
                        act.wait_ge(T2.sem, T2.at("o", t - 1))
                    for c in range(2):
                        act.wait_ge(T2.sem, T2.at(f"p{c}", t))
                        act.activation(pT[:, c, :, :], tp[c][:, :, :], ACT.Copy).then_inc(A2.sem, 1)

                def norm(t, u, n):
                    def free():
                        if not early(t, 1):
                            act.wait_ge(T3.sem, T3.at("n1", t - 1))
                    norm_act(act, A3, lambda: act.wait_ge(V2.sem, V2.at("r1", t)), x2[0:n, u, :], sq, ss,
                             xn[0:n, :], t, n, pr.eps, free)
                lagged(act, [score, apply, norm])

            @block.vector
            def _(dve):
                def score(t, u, n):
                    if n == NS:
                        return
                    dve.wait_ge(T1.sem, T1.at("s1", t))
                    for c in range(2):
                        last = dve.tensor_reduce(top[:, u, 2 * c:2 * c + 2], s_ps[c][:, :, :], AX.X, ALU.max)
                    last.then_inc(V1.sem, 1)
                    dve.wait_ge(V1.sem, V1.at("top", t))
                    dve.tensor_scalar(top[:, u, :], top[:, u, :], -1.0, None, ALU.mult).then_inc(V1.sem, 1)

                def apply(t, u, n):
                    if n == P:
                        dve.wait_ge(A1.sem, A1.at("exp", t))
                        dve.reciprocal(den[:, u, :], den[:, u, :]).then_inc(V2.sem, 1)
                        dve.wait_ge(V2.sem, V2.at("inv", t))
                        dve.tensor_tensor(prob[:, u, :, :], prob[:, u, :, :], bc(den[:, u, :], MEM), ALU.mult)\
                           .then_inc(V2.sem, 1)
                        dve.wait_ge(T2.sem, T2.at("o", t))
                        if not early(t, 1):
                            dve.wait_ge(T2.sem, T2.at("y1", t - 1))
                        dve.tensor_copy(oT[:, :, :], o_ps[:, :, :]).then_inc(V2.sem, 1)
                    else:
                        for _ in range(3):
                            dve.engine_nop().then_inc(V2.sem, 1)
                    if not early(t):
                        dve.wait_ge(stored[u], (t - u) * 8)
                        dve.wait_ge(A3.sem, A3.at("scaled", t - 2))
                    dve.wait_ge(loaded[u], (t - u) * 8 + 16)
                    for c in range(2):
                        dve.wait_ge(T2.sem, T2.at(f"y{c}", t) if n == P else T2.at("p0", t) + c)
                        dve.tensor_tensor(x2[0:n, u, c * 512:(c + 1) * 512], y[c][0:n, :],
                                          x1[0:n, u, c * 512:(c + 1) * 512], ALU.add).then_inc(V2.sem, 1)

                def norm(t, u, n):
                    for c in range(2):
                        dve.wait_ge(T3.sem, T3.at(f"n{c}", t))
                        dve.tensor_tensor(hT[:, 4 * c:4 * c + 4, bass.ds(t * P, n)], tp[c][:, :, 0:n],
                                          bc(g_ffn[:, 4 * c:4 * c + 4], n), ALU.mult).then_inc(V3.sem, 1)
                lagged(dve, [score, apply, norm])


def ffn_in(nc, pr, hT, taps, bias, state_in, saved):
    w = pr.i["ffn_w_in"][0].rearrange("(k p) n -> p k n", p=P)
    with Stage(nc) as st:
        W = st.sb("W", [P, 2, 2, KD, P])
        raw_p = st.sb("raw_p", [P, 2 + SEQ])
        raw_s = st.sb("raw_s", [P, NB, 2 + NQ])
        val = st.sb("val", [P, 2, TOK])
        mix = st.sb("mix", [P, TOK])
        out = st.sb("out", [P, 2, TOK])
        acc = [st.ps(f"acc{j}", [P, 512]) for j in range(5)]
        w_in = [st.sem(f"w_in{u}") for u in range(2)]
        stored = [st.sem(f"stored{u}") for u in range(2)]
        cleared = st.sem("halo_cleared")
        order = [f"{x}{c}" for c in range(NCH) for x in "gv"]
        T = st.steps("pe_steps", " ".join(order))
        A = st.steps("act_steps", " ".join(order) + " halo silu")
        V = st.steps("dve_steps", "a b c saved product")
        with nc.Block() as block:
            @block.sync
            def _(sp):
                def load(t, u):
                    if not early(t):
                        sp.wait_ge(T.sem, T.at(order[-1], t - 2))
                    for x in range(2):
                        sp.dma_start(W[:, u, x, :, :], w[:, :, bass.ds(t * P + x * D_FF, P)]).then_inc(w_in[u], 16)

                def store(t, u):
                    sp.wait_ge(V.sem, V.at("product", t))
                    sp.dma_start(pr.act_t[bass.ds(t, 1), :, :].rearrange("a p n -> p (a n)"), out[:, u, :])\
                      .then_inc(stored[u], 16)

                def body(t, u):
                    load(t, u)
                    if not early(t, 1):
                        store(t - 1, 1 - u)
                sweep(sp, FB, body)
                store(FB - 1, (FB - 1) % 2)
                for u in range(2):
                    sp.wait_ge(stored[u], 16 * (FB // 2))

            @block.tensor
            def _(pe):
                def body(t, u):
                    pe.wait_ge(w_in[u], (t - u) * 16 + 32)
                    for j, name in enumerate(order):
                        if j >= 5:
                            pe.wait_ge(A.sem, A.at(order[j - 5], t))
                        elif not early(t, 1):
                            pe.wait_ge(A.sem, A.at(order[j + 5], t - 1))
                        c = j // 2
                        for k in range(KD):
                            mm = pe.matmul(acc[j % 5][:, 0:CH], W[:, u, j % 2, k, :], hT[:, k, c * CH:(c + 1) * CH],
                                           start=(k == 0), stop=(k == KD - 1))
                        mm.then_inc(T.sem, 1)
                sweep(pe, FB, body)

            @block.scalar
            def _(act):
                def body(t, u):
                    if not early(t, 1):
                        act.wait_ge(V.sem, V.at("saved", t - 1))
                    if not early(t):
                        act.wait_ge(V.sem, V.at("product", t - 2))
                    for j, name in enumerate(order):
                        c = j // 2
                        n = CH if c < NCH - 1 else LASTP
                        act.wait_ge(T.sem, T.at(name, t))
                        if j % 2:
                            last = act.activation(val[:, u, c * CH:(c + 1) * CH], acc[j % 5][:, 0:CH], ACT.Copy)
                        else:
                            last = act.activation(raw_p[:, 2 + c * CH:2 + c * CH + n], acc[j % 5][:, 0:n], ACT.Copy)
                            if c == NCH - 1:
                                last = act.activation(raw_s[:, :, 2:2 + NQ], acc[j % 5][:, n:CH].rearrange(
                                    "p (b q) -> p b q", q=NQ), ACT.Copy)
                        last.then_inc(A.sem, 1)
                    act.activation(raw_s[:, :, 0:2], state_in[:, bass.ds(t, 1), :].rearrange(
                        "p a (b j) -> p (a b) j", j=2), ACT.Copy).then_inc(A.sem, 1)
                    act.wait_ge(V.sem, V.at("c", t))
                    if not early(t):
                        act.wait_ge(stored[u], (t - u) * 8)
                    act.activation(out[:, u, :], mix[:, :], ACT.Silu,
                                   bias=bias[:, bass.ds(t, 1)]).then_inc(A.sem, 1)
                sweep(act, FB, body)

            @block.vector
            def _(dve):
                dve.memset(raw_p[:, 0:2], 0.0).then_inc(cleared, 1)
                dve.wait_ge(cleared, 1)

                def body(t, u):
                    dve.wait_ge(A.sem, A.at("halo", t))
                    if not early(t, 1):
                        dve.wait_ge(A.sem, A.at("silu", t - 1))
                    mp, ms = mix[:, 0:SEQ], mix[:, SEQ:TOK].rearrange("p (b q) -> p b q", q=NQ)
                    for j in range(3):
                        tap = taps[:, bass.ds(t, 1), j:j + 1].rearrange("p a b -> p (a b)")
                        rp, rs = raw_p[:, j:j + SEQ], raw_s[:, :, j:j + NQ]
                        if j == 0:
                            dve.tensor_scalar(ms, rs, tap, None, ALU.mult)
                            dve.tensor_scalar(mp, rp, tap, None, ALU.mult).then_inc(V.sem, 1)
                        else:
                            dve.wait_ge(V.sem, V.at("ab"[j - 1], t))
                            dve.scalar_tensor_tensor(ms, rs, tap, ms, ALU.mult, ALU.add)
                            dve.scalar_tensor_tensor(mp, rp, tap, mp, ALU.mult, ALU.add).then_inc(V.sem, 1)
                    dve.tensor_copy(saved[:, bass.ds(t, 1), 0:2], raw_p[:, SEQ:SEQ + 2].unsqueeze(1))
                    dve.tensor_copy(saved[:, bass.ds(t, 1), 2:2 * (NB + 1)].rearrange(
                        "p a (b j) -> p (a b) j", j=2), raw_s[:, :, NQ:NQ + 2]).then_inc(V.sem, 1)
                    dve.wait_ge(A.sem, A.at("silu", t))
                    dve.tensor_tensor(out[:, u, :], out[:, u, :], val[:, u, :], ALU.mult).then_inc(V.sem, 1)
                sweep(dve, FB, body)


def ffn_out(nc, pr, y_rows, g_final):
    with Stage(nc) as st:
        w = st.sb("w", [P, FB, D])
        a = st.sb("a", [P, 2, FB, P])
        x2 = st.sb("x2", [P, 2, D])
        x3 = st.sb("x3", [P, D])
        sq = st.sb("sq", [P, D])
        ss = st.sb("ss", [P, 1])
        xn = st.sb("xn", [P, D])
        res = st.sb("res", [P, 2, D])
        y = [[st.ps(f"y{u}{c}", [P, 512]) for c in range(2)] for u in range(2)]
        w_in = st.sem("w_in")
        loaded = [st.sem(f"loaded{u}") for u in range(2)]
        stored = [st.sem(f"stored{u}") for u in range(2)]
        T = st.steps("pe_steps", "m0 m1")
        V = st.steps("dve_steps", "r0 r1 gain")
        A = st.steps("act_steps", "square log rstd scaled")
        with nc.Block() as block:
            @block.sync
            def _(sp):
                sp.dma_start(w[:, :, :], pr.i["ffn_w_out"][0].rearrange("(k p) n -> p k n", p=P)).then_inc(w_in, 16)

                def load(t, u, n):
                    if not early(t):
                        sp.wait_ge(V.sem, V.at("r1", t - 2))
                    sp.dma_start(a[:, u, :, 0:n], pr.act_t.rearrange("f p n -> p f n")[:, :, bass.ds(t * P, n)])\
                      .then_inc(loaded[u], 16)
                    sp.dma_start(x2[0:n, u, :], rows(pr.x2, t, n)).then_inc(loaded[u], 16)

                def store(t, u, n):
                    sp.wait_ge(V.sem, V.at("gain", t))
                    sp.dma_start(y_rows(t, n), res[0:n, u, :]).then_inc(stored[u], 16)
                lagged(sp, [load, store])
                sp.wait_ge(stored[0], 16 * 9)
                sp.wait_ge(stored[1], 16 * 8)

            @block.tensor
            def _(pe):
                pe.wait_ge(w_in, 16)

                def out(t, u, n):
                    pe.wait_ge(loaded[u], (t - u) * 16 + 32)
                    for c in range(2):
                        if not early(t):
                            pe.wait_ge(V.sem, V.at(f"r{c}", t - 2))
                        for k in range(FB):
                            mm = pe.matmul(y[u][c][0:n, :], a[:, u, k, 0:n], w[:, k, c * 512:(c + 1) * 512],
                                           start=(k == 0), stop=(k == FB - 1))
                        mm.then_inc(T.sem, 1)
                lagged(pe, [out])

            @block.vector
            def _(dve):
                def fin(t, u, n):
                    if not early(t, 1):
                        dve.wait_ge(A.sem, A.at("scaled", t - 1))
                    for c in range(2):
                        dve.wait_ge(T.sem, T.at(f"m{c}", t))
                        dve.tensor_tensor(x3[0:n, c * 512:(c + 1) * 512], y[u][c][0:n, :],
                                          x2[0:n, u, c * 512:(c + 1) * 512], ALU.add).then_inc(V.sem, 1)
                    dve.wait_ge(A.sem, A.at("scaled", t))
                    if not early(t):
                        dve.wait_ge(stored[u], (t - u) * 8)
                    dve.tensor_tensor(res[0:n, u, :], xn[0:n, :], g_final[0:n, :], ALU.mult).then_inc(V.sem, 1)
                lagged(dve, [fin])

            @block.scalar
            def _(act):
                def fin(t, u, n):
                    def free():
                        if not early(t, 1):
                            act.wait_ge(V.sem, V.at("gain", t - 1))
                    norm_act(act, A, lambda: act.wait_ge(V.sem, V.at("r1", t)), x3[0:n, :], sq, ss, xn[0:n, :],
                             t, n, pr.eps, free)
                lagged(act, [fin])


def mem_sample(nc, pr, hT, o_out):
    with Stage(nc) as st:
        wq = st.sb("wq", [P, KD, MI])
        K = st.sb("K", [P, 2, 2, MI])
        V_ = st.sb("V", [P, NB, 2, MI])
        kT = st.sb("kT", [P, 2, MH, P])
        qT = st.sb("qT", [P, MH, NS])
        sT = st.sb("sT", [P, 2, NB, MH, NQ])
        s = st.sb("s", [P, 2, P])
        top, den = st.sb("top", [P, 1]), st.sb("den", [P, 1])
        pT = st.sb("pT", [P, 2, NB, MH, NQ])
        q_ps = st.ps("q_ps", [P, MH, NS])
        k_ps = [st.ps(f"k_ps{c}", [P, 4, P]) for c in range(2)]
        s_ps = st.ps("s_ps", [P, 2, NB, MH, NQ])
        t_ps = st.ps("t_ps", [P, 2, P])
        r_ps = st.ps("r_ps", [P, 2, P])
        o_ps = st.ps("o_ps", [P, NB, MH, NQ])
        w_in, v_in = st.sem("w_in"), st.sem("v_in")
        k_in = [st.sem(f"k_in{u}") for u in range(2)]
        q_done, q_copied = st.sem("q_done"), st.sem("q_copied")
        T = st.steps("pe_keys", "k0 k1 s")
        A = st.steps("act_keys", "k0 k1")
        fin_pe, fin_dve, fin_act = st.sem("fin_pe"), st.sem("fin_dve"), st.sem("fin_act")
        with nc.Block() as block:
            @block.sync
            def _(sp):
                sp.dma_start(wq[:, :, :], pr.i["mem_wq"][0].rearrange("(k p) n -> p k n", p=P)).then_inc(w_in, 16)
                for b in range(NB):
                    u = b % 2
                    if b >= 2:
                        sp.wait_ge(T.sem, T.at("k1", b - 2))
                    sp.dma_start(K[:, u, :, :], pr.i["cache_mem_k"][0, b].rearrange("(c p) h d -> p c (h d)", p=P))\
                      .then_inc(k_in[u], 16)
                    sp.dma_start(V_[:, b, :, :], pr.i["cache_mem_v"][0, b].rearrange("(c p) h d -> p c (h d)", p=P))\
                      .then_inc(v_in, 16)

            @block.tensor
            def _(pe):
                pe.wait_ge(w_in, 16)
                for h in range(MH):
                    for k in range(KD):
                        mm = pe.matmul(q_ps[:, h, :], wq[:, k, h * P:(h + 1) * P], hT[:, k, SEQ:TOK],
                                       start=(k == 0), stop=(k == KD - 1))
                mm.then_inc(q_done, 1)
                pe.wait_ge(q_copied, 1)
                for b in range(NB):
                    u = b % 2
                    pe.wait_ge(k_in[u], 16 * (b // 2 + 1))
                    for c in range(2):
                        if b >= 1:
                            pe.wait_ge(A.sem, A.at(f"k{c}", b - 1))
                        for h in range(MH):
                            mm = pe.transpose(k_ps[c][:, h, :], K[:, u, c, h * P:(h + 1) * P], pr.ident[:, :])
                        mm.then_inc(T.sem, 1)
                    for c in range(2):
                        pe.wait_ge(A.sem, A.at(f"k{c}", b))
                        for h in range(MH):
                            mm = pe.matmul(s_ps[:, c, b, h, :], kT[:, c, h, :], qT[:, h, b * NQ:(b + 1) * NQ],
                                           start=True, stop=True)
                    mm.then_inc(T.sem, 1)
                pe.wait_ge(fin_dve, 1)
                for c in range(2):
                    mm = pe.transpose(t_ps[:, c, :], sT[:, c, :, :, :].rearrange("p b h q -> p (b h q)"), pr.ident[:, :])
                mm.then_inc(fin_pe, 1)
                pe.wait_ge(fin_dve, 5)
                for c in range(2):
                    mm = pe.transpose(r_ps[:, c, :], s[:, c, :], pr.ident[:, :])
                mm.then_inc(fin_pe, 1)
                pe.wait_ge(fin_dve, 6)
                pe.wait_ge(v_in, 16 * NB)
                for b in range(NB):
                    for h in range(MH):
                        for c in range(2):
                            mm = pe.matmul(o_ps[:, b, h, :], V_[:, b, c, h * P:(h + 1) * P], pT[:, c, b, h, :],
                                           start=(c == 0), stop=(c == 1))
                mm.then_inc(fin_pe, 1)

            @block.scalar
            def _(act):
                act.wait_ge(q_done, 1)
                act.activation(qT[:, :, :], q_ps[:, :, :], ACT.Copy, scale=float(MHD) ** -0.5).then_inc(q_copied, 1)
                for b in range(NB):
                    if b >= 1:
                        act.wait_ge(T.sem, T.at("s", b - 1))
                    for c in range(2):
                        act.wait_ge(T.sem, T.at(f"k{c}", b))
                        act.activation(kT[:, c, :, :], k_ps[c][:, :, :], ACT.Copy).then_inc(A.sem, 1)
                act.wait_ge(fin_dve, 3)
                act.activation(s[:, :, :], t_ps[:, :, :], ACT.Exp, bias=top[:, :], accum_out=den[:, :])\
                   .then_inc(fin_act, 1)

            @block.vector
            def _(dve):
                dve.wait_ge(T.sem, T.at("s", NB - 1))
                dve.tensor_copy(sT[:, :, :, :, :].rearrange("p c b h q -> p (c b h q)"),
                                s_ps[:, :, :, :, :].rearrange("p c b h q -> p (c b h q)")).then_inc(fin_dve, 1)
                dve.wait_ge(fin_pe, 1)
                dve.tensor_reduce(top[:, :], t_ps[:, :, :].rearrange("p c m -> p (c m)"), AX.X, ALU.max)\
                   .then_inc(fin_dve, 1)
                dve.wait_ge(fin_dve, 2)
                dve.tensor_scalar(top[:, :], top[:, :], -1.0, None, ALU.mult).then_inc(fin_dve, 1)
                dve.wait_ge(fin_act, 1)
                dve.reciprocal(den[:, :], den[:, :]).then_inc(fin_dve, 1)
                dve.wait_ge(fin_dve, 4)
                dve.tensor_scalar(s[:, :, :], s[:, :, :], den[:, 0:1], None, ALU.mult).then_inc(fin_dve, 1)
                dve.wait_ge(fin_pe, 2)
                dve.tensor_copy(pT[:, :, :, :, :].rearrange("p c b h q -> p (c b h q)"),
                                r_ps[:, :, :].rearrange("p c m -> p (c m)")).then_inc(fin_dve, 1)
                dve.wait_ge(fin_pe, 3)
                dve.tensor_copy(o_out.rearrange("p h (b q) -> p b h q", q=NQ), o_ps[:, :, :, :]).then_inc(fin_dve, 1)


def diff_rows(nc, pr, k_rows, v_rows):
    with Stage(nc) as st:
        c = st.sb("cols", [P, 2, 4, P])
        r = st.sb("rows", [P, 2, 4 * P])
        tp = [st.ps(f"tp{u}", [P, 4 * P]) for u in range(2)]
        loaded = [st.sem(f"loaded{u}") for u in range(2)]
        stored = [st.sem(f"stored{u}") for u in range(2)]
        T, V = st.steps("pe_steps", "t"), st.steps("dve_steps", "copy")
        with nc.Block() as block:
            @block.sync
            def _(sp):
                def load(t, u, n):
                    if not early(t):
                        sp.wait_ge(T.sem, T.at("t", t - 2))
                    sp.dma_start(c[:, u, :, 0:n], pr.cols.rearrange("f p n -> p f n")[
                        :, B_DIFF + 2:B_DIFF + 6, bass.ds(t * P, n)]).then_inc(loaded[u], 16)

                def store(t, u, n):
                    sp.wait_ge(V.sem, V.at("copy", t))
                    sp.dma_start(k_rows(t, n), r[0:n, u, 0:W_B]).then_inc(stored[u], 16)
                    sp.dma_start(v_rows(t, n), r[0:n, u, W_B:2 * W_B]).then_inc(stored[u], 16)
                lagged(sp, [load, store])
                sp.wait_ge(stored[0], 32 * 9)
                sp.wait_ge(stored[1], 32 * 8)

            @block.tensor
            def _(pe):
                def flip(t, u, n):
                    pe.wait_ge(loaded[u], (t - u) * 8 + 16)
                    if not early(t):
                        pe.wait_ge(V.sem, V.at("copy", t - 2))
                    for j in range(4):
                        mm = pe.transpose(tp[u][0:n, j * P:(j + 1) * P], c[:, u, j, 0:n], pr.ident[:, :])
                    mm.then_inc(T.sem, 1)
                lagged(pe, [flip])

            @block.vector
            def _(dve):
                def copy(t, u, n):
                    dve.wait_ge(T.sem, T.at("t", t))
                    if not early(t):
                        dve.wait_ge(stored[u], (t - u) * 16)
                    dve.tensor_copy(r[0:n, u, :], tp[u][0:n, :]).then_inc(V.sem, 1)
                lagged(dve, [copy])


def diff_prompt(nc, pr, v_out, causal, neg_lam):
    for g in range(4):
        diff_prompt_group(nc, pr, v_out, causal, neg_lam, g)


def diff_prompt_group(nc, pr, v_out, causal, neg_lam, g):
    NC, KT, ITEMS = g + 1, 4 * (g + 1), 16
    E = 512 * NC
    scale = float(DB) ** -0.5
    with Stage(nc) as st:
        k = st.sb("k", [DB, 2, 2, E])
        q = st.sb("q", [DB, 2, 2, P])
        v = st.sb("v", [P, 2, KT, HD])
        prob = st.sb("prob", [P, 2, 2, E])
        w = st.sb("w", [P, 2, E])
        wT = st.sb("wT", [P, 2, 4, P])
        top = st.sb("top", [P, 2, 2])
        den = st.sb("den", [P, 2, 2, NC])
        inv = st.sb("inv", [P, 2, 2])
        o = st.sb("o", [P, 2, HD])
        s_ps = st.ps("s_ps", [P, 4, 512])
        tp = [st.ps(f"tp{j}", [P, 4, P]) for j in range(2)]
        o_ps = [st.ps(f"o_ps{u}", [P, 512]) for u in range(2)]
        loaded = [st.sem(f"loaded{u}") for u in range(2)]
        stored = [st.sem(f"stored{u}") for u in range(2)]
        T1, T2 = st.steps("pe_score", "s0 s1"), st.steps("pe_apply", " ".join(f"t{c}" for c in range(NC)) + " o")
        A1 = st.steps("act_exp", " ".join(f"e{m}{c}" for m in range(2) for c in range(NC)) + " scaled")
        A2 = st.steps("act_apply", " ".join(f"t{c}" for c in range(NC)))
        V1 = st.steps("dve_top", "mask0 top0 neg0 mask1 top1 neg1 den inv lam w")
        V2 = st.steps("dve_out", "o")

        def items(eng, parts):
            def step(t, u):
                for j, part in enumerate(parts):
                    if early(t, j):
                        break
                    part(t - j, (u + j) % 2)
            sweep(eng, ITEMS, step)
            for t in range(ITEMS, ITEMS + len(parts) - 1):
                for j, part in enumerate(parts):
                    if t - j < ITEMS:
                        part(t - j, (t - j) % 2)

        with nc.Block() as block:
            @block.sync
            def _(sp):
                def load(t, u):
                    h, j = t // 4, t % 4
                    if not early(t):
                        sp.wait_ge(T2.sem, T2.at("o", t - 2))
                    flat = pr.cols.rearrange("f p n -> (f p) n")
                    sp.dma_start(k[:, u, :, :], flat[bass.ds(h * HD + (B_DIFF + 2) * P, HD), 0:E].rearrange(
                        "(m d) n -> d m n", d=DB)).then_inc(loaded[u], 16)
                    sp.dma_start(q[:, u, :, :], flat[bass.ds(h * HD + B_DIFF * P, HD),
                                                     bass.ds(j * P + g * 512, P)].rearrange(
                        "(m d) n -> d m n", d=DB)).then_inc(loaded[u], 16)
                    sp.dma_start(v[:, u, :, :], v_out.rearrange("(c p) n -> p c n", p=P)[
                        :, 0:KT, bass.ds(h * HD, HD)]).then_inc(loaded[u], 16)

                def store(t, u):
                    h, j = t // 4, t % 4
                    sp.wait_ge(V2.sem, V2.at("o", t))
                    sp.dma_start(pr.o_raw[bass.ds(j * P + g * 512, P), bass.ds(h * HD + W_A, HD)], o[:, u, :])\
                      .then_inc(stored[u], 16)
                items(sp, [load, store])
                for u in range(2):
                    sp.wait_ge(stored[u], 16 * (ITEMS // 2))

            @block.tensor
            def _(pe):
                def score(t, u):
                    pe.wait_ge(loaded[u], (t - u) * 24 + 48)
                    for m in range(2):
                        for c in range(NC):
                            if m == 1:
                                pe.wait_ge(A1.sem, A1.at(f"e0{c}", t))
                            elif not early(t, 1):
                                pe.wait_ge(A1.sem, A1.at(f"e1{c}", t - 1))
                            mm = pe.matmul(s_ps[:, c, :], q[:, u, m, :], k[:, u, m, c * 512:(c + 1) * 512],
                                           start=True, stop=True)
                        mm.then_inc(T1.sem, 1)

                def apply(t, u):
                    pe.wait_ge(V1.sem, V1.at("w", t))
                    if not early(t):
                        pe.wait_ge(V2.sem, V2.at("o", t - 2))
                    def flip(c):
                        if c >= 2:
                            pe.wait_ge(A2.sem, A2.at(f"t{c - 2}", t))
                        elif not early(t, 1):
                            pe.wait_ge(A2.sem, A2.at(f"t{NC - 1}", t - 1))
                        for j in range(4):
                            mm = pe.transpose(tp[c % 2][:, j, :], w[:, u, (4 * c + j) * P:(4 * c + j + 1) * P],
                                              pr.ident[:, :])
                        mm.then_inc(T2.sem, 1)
                    for c in range(NC):
                        flip(c)
                        if c >= 1:
                            use(t, u, c - 1)
                    use(t, u, NC - 1).then_inc(T2.sem, 1)

                def use(t, u, c):
                    pe.wait_ge(A2.sem, A2.at(f"t{c}", t))
                    for j in range(4):
                        kt = 4 * c + j
                        mm = pe.matmul(o_ps[u][:, 0:HD], wT[:, c % 2, j, :], v[:, u, kt, :],
                                       start=(kt == 0), stop=(kt == KT - 1))
                    return mm
                items(pe, [score, apply])

            @block.scalar
            def _(act):
                def exps(t, u):
                    for m in range(2):
                        act.wait_ge(V1.sem, V1.at(f"neg{m}", t))
                        if m == 0 and not early(t):
                            act.wait_ge(V1.sem, V1.at("w", t - 2))
                        for c in range(NC):
                            act.activation(prob[:, u, m, c * 512:(c + 1) * 512], s_ps[:, c, :], ACT.Exp, scale=scale,
                                           bias=top[:, u, m:m + 1], accum_out=den[:, u, m, c:c + 1])\
                               .then_inc(A1.sem, 1)
                    act.wait_ge(V1.sem, V1.at("lam", t))
                    act.activation(prob[:, u, 1, :], prob[:, u, 1, :], ACT.Copy, scale=inv[:, u, 1:2])\
                       .then_inc(A1.sem, 1)

                def apply(t, u):
                    for c in range(NC):
                        act.wait_ge(T2.sem, T2.at(f"t{c}", t))
                        if c >= 2:
                            act.wait_ge(T2.sem, T2.at(f"t{c}", t))
                        elif not early(t, 1):
                            act.wait_ge(T2.sem, T2.at("o", t - 1))
                        act.activation(wT[:, c % 2, :, :], tp[c % 2][:, :, :], ACT.Copy).then_inc(A2.sem, 1)
                items(act, [exps, apply])

            @block.vector
            def _(dve):
                def top_(t, u):
                    for m in range(2):
                        dve.wait_ge(T1.sem, T1.at(f"s{m}", t))
                        dve.tensor_tensor(s_ps[:, NC - 1, :], s_ps[:, NC - 1, :],
                                          causal[:, bass.ds(t % 4, 1), :].rearrange("p a n -> p (a n)"), ALU.add)\
                           .then_inc(V1.sem, 1)
                        dve.wait_ge(V1.sem, V1.at(f"mask{m}", t))
                        dve.tensor_reduce(top[:, u, m:m + 1], s_ps[:, 0:NC, :].rearrange("p c n -> p (c n)"),
                                          AX.X, ALU.max).then_inc(V1.sem, 1)
                        dve.wait_ge(V1.sem, V1.at(f"top{m}", t))
                        dve.tensor_scalar(top[:, u, m:m + 1], top[:, u, m:m + 1], -scale, None, ALU.mult)\
                           .then_inc(V1.sem, 1)
                    dve.wait_ge(A1.sem, A1.at(f"e1{NC - 1}", t))
                    dve.tensor_reduce(inv[:, u, :], den[:, u, :, :], AX.X, ALU.add).then_inc(V1.sem, 1)
                    dve.wait_ge(V1.sem, V1.at("den", t))
                    dve.reciprocal(inv[:, u, :], inv[:, u, :]).then_inc(V1.sem, 1)
                    dve.wait_ge(V1.sem, V1.at("inv", t))
                    dve.tensor_tensor(inv[:, u, 1:2], inv[:, u, 1:2], neg_lam[:, :], ALU.mult).then_inc(V1.sem, 1)
                    dve.wait_ge(A1.sem, A1.at("scaled", t))
                    if not early(t):
                        dve.wait_ge(T2.sem, T2.at("o", t - 2))
                    dve.scalar_tensor_tensor(w[:, u, :], prob[:, u, 0, :], inv[:, u, 0:1], prob[:, u, 1, :],
                                             ALU.mult, ALU.add).then_inc(V1.sem, 1)

                def out(t, u):
                    dve.wait_ge(T2.sem, T2.at("o", t))
                    if not early(t):
                        dve.wait_ge(stored[u], (t - u) * 8)
                    dve.tensor_copy(o[:, u, :], o_ps[u][:, 0:HD]).then_inc(V2.sem, 1)
                items(dve, [top_, out])


def diff_paged(nc, pr, k_new, v_new, seqm, neg_lam, new_mask):
    GP, G = 4, PAGES // 4
    NPG = PAGES + 1
    scale = float(DB) ** -0.5
    kp, vp = pr.i["cache_diff_k"][0], pr.i["cache_diff_v"][0]
    n_pool = kp.shape[0]
    with Stage(nc) as st:
        table = st.sb("table", [1, NB * PAGES], I32)
        qT = st.sb("qT", [P, 2, NS])
        qd = st.sb("qd", [P, NB, 2, 16])
        K = st.sb("K", [P, 4, GP, W_B])
        V_ = st.sb("V", [P, PAGES, W_B])
        kn = st.sb("kn", [P, W_B])
        vn = st.sb("vn", [P, W_B])
        kT = st.sb("kT", [P, 2, 2, GP, P])
        S = st.sb("S", [P, NPG, 32])
        top = st.sb("top", [P, 32])
        topT = st.sb("topT", [32, 1])
        diag = st.sb("diag", [32, 32])
        sums = st.sb("sums", [P, 32])
        rden = st.sb("rden", [32, 1])
        comb = st.sb("comb", [32, H_B, HD])
        O = st.sb("O", [32, W_B])
        og = st.sb("og", [NQ, W_B])
        t_ps = [st.ps(f"t_ps{h}", [P, GP, P]) for h in range(2)]
        s_ps = [st.ps(f"s_ps{u}", [P, GP, 32]) for u in range(2)]
        m_ps = st.ps("m_ps", [P, 512])
        b_ps = st.ps("b_ps", [P, 512])
        o_ps = st.ps("o_ps", [P, 512])
        f_ps = st.ps("f_ps", [P, 512])
        init, mem0 = st.sem("init"), st.sem("zeroed")
        k_in = [st.sem(f"k_in{j}") for j in range(4)]
        v_in, n_in, o_out = st.sem("v_in"), st.sem("new_in"), st.sem("o_out")
        groups = [f"g{g}" for g in range(G)] + ["gn"]
        T = st.steps("pe_steps", " ".join(f"t{x} s{x}" for x in groups) + " topT topB den pv fin")
        A = st.steps("act_steps", " ".join(groups) + " exp")
        V = st.steps("dve_steps", " ".join(f"k{x} s{x}" for x in groups)
                     + " newmask top topT diag sub sums rden comb O og")
        late = lambda S_, name, b: S_.at(name, b + 1)
        with nc.Block() as block:
            @block.sync
            def _(sp):
                sp.dma_start(table[:, :], pr.i["page_table"].rearrange("(a b) n -> a (b n)", a=1)).then_inc(init, 16)
                sp.dma_start(qT[:, :, :], pr.cols.rearrange("f p n -> p f n")[:, B_DIFF:B_DIFF + 2, SEQ:TOK])\
                  .then_inc(init, 16)
                sp.wait_ge(init, 32)
                sp.wait_ge(mem0, 4)
                sp.nop().then_inc(o_out, 16)
                with sp.Fori(0, NB) as b:
                    for g in range(G):
                        j = g % 4
                        sp.wait_ge(T.sem, late(T, f"tg{g - 4}", b) if g >= 4 else late(T, f"tg{G + g - 4}", b - 1))
                        for i in range(GP):
                            page = sp.value_load(table[0:1, bass.ds(b * PAGES + (g * GP + i), 1)],
                                                 min_val=0, max_val=n_pool - 1)
                            sp.dma_start(K[:, j, i, :], kp[bass.ds(page, 1)].rearrange("a p h d -> p (a h d)"))\
                              .then_inc(k_in[j], 16)
                    sp.wait_ge(T.sem, late(T, "fin", b - 1))
                    sp.dma_start(kn[0:NQ, :], k_new[bass.ds(b * NQ, NQ), :]).then_inc(n_in, 16)
                    sp.dma_start(vn[0:NQ, :], v_new[bass.ds(b * NQ, NQ), :]).then_inc(n_in, 16)
                    sp.wait_ge(V.sem, late(V, "og", b))
                    sp.dma_start(pr.o_raw[bass.ds(b * NQ + SEQ, NQ), W_A:W_A + W_B], og[:, :]).then_inc(o_out, 16)
                sp.wait_ge(o_out, 16 * NB + 16)

            @block.gpsimd
            def _(pool):
                pool.memset(kn[:, :], 0.0).then_inc(mem0, 1)
                pool.memset(vn[:, :], 0.0).then_inc(mem0, 1)
                pool.memset(qd[:, :, :, :], 0.0).then_inc(mem0, 1)
                pool.memset(comb[:, :, :], 0.0).then_inc(mem0, 1)
                pool.wait_ge(init, 32)
                with pool.Fori(0, NB) as b:
                    pool.wait_ge(T.sem, late(T, "pv", b - 1))
                    for i in range(PAGES):
                        page = pool.value_load(table[0:1, bass.ds(b * PAGES + i, 1)], min_val=0, max_val=n_pool - 1)
                        pool.dma_start(V_[:, i, :], vp[bass.ds(page, 1)].rearrange("a p h d -> p (a h d)"))\
                            .then_inc(v_in, 16)

            @block.tensor
            def _(pe):
                pe.nop().then_inc(T.sem, len(T.names))
                pe.wait_ge(V.sem, len(V.names))
                with pe.Fori(0, NB) as b:
                    def scores(x, g, last):
                        n = GP if x != "gn" else 1
                        pe.wait_ge(A.sem, late(A, x, b))
                        pe.wait_ge(V.sem, late(V, f"k{x}", b))
                        pe.wait_ge(V.sem, late(V, f"s{groups[g - 2]}", b) if g >= 2
                                   else late(V, f"s{groups[len(groups) - 1 - (g + len(groups)) % 2]}", b - 1))
                        for i in range(n):
                            for h in range(2):
                                mm = pe.matmul(s_ps[g % 2][:, i, 16 * h:16 * h + 16], kT[:, g % 2, h, i, :],
                                               qd[:, bass.ds(b, 1), h, :].rearrange("p a n -> p (a n)"),
                                               start=True, stop=True)
                        mm.then_inc(T.sem, 1)

                    for g, x in enumerate(groups):
                        n = GP if x != "gn" else 1
                        if x != "gn":
                            pe.wait_ge(k_in[g % 4], b * (16 * G) + 64 * (g // 4 + 1))
                        else:
                            pe.wait_ge(n_in, b * 32 + 32)
                        prev = (A, groups[g - 1], b) if g else (A, groups[-1], b - 1)
                        pe.wait_ge(A.sem, late(*prev))
                        pe.wait_ge(V.sem, late(V, "k" + prev[1], prev[2]))
                        for h in range(2):
                            for i in range(n):
                                src = (K[:, g % 4, i, h * P:(h + 1) * P] if x != "gn" else kn[:, h * P:(h + 1) * P])
                                mm = pe.transpose(t_ps[h][:, i, :], src, pr.ident[:, :])
                        mm.then_inc(T.sem, 1)
                        scores(x, g, False)
                    pe.wait_ge(V.sem, late(V, "top", b))
                    pe.transpose(m_ps[0:32, 0:P], top[:, :], pr.ident[:, :]).then_inc(T.sem, 1)
                    pe.wait_ge(V.sem, late(V, "diag", b))
                    pe.matmul(b_ps[:, 0:32], pr.ones[0:32, :], diag[:, :], start=True, stop=True).then_inc(T.sem, 1)
                    pe.wait_ge(V.sem, late(V, "sums", b))
                    pe.matmul(m_ps[0:32, 256:257], sums[:, :], pr.ones[:, 0:1], start=True, stop=True).then_inc(T.sem, 1)
                    pe.wait_ge(v_in, b * (16 * PAGES) + 16 * PAGES)
                    for i in range(NPG):
                        mm = pe.matmul(o_ps[0:32, 0:W_B], S[:, i, :], V_[:, i, :] if i < PAGES else vn[:, :],
                                       start=(i == 0), stop=(i == NPG - 1))
                    mm.then_inc(T.sem, 1)
                    pe.wait_ge(V.sem, late(V, "O", b))
                    for h in range(H_B):
                        mm = pe.matmul(f_ps[0:HD, h * HD:(h + 1) * HD], comb[:, h, :],
                                       O[:, h * HD:(h + 1) * HD], start=True, stop=True)
                    mm.then_inc(T.sem, 1)

            @block.scalar
            def _(act):
                act.nop().then_inc(A.sem, len(A.names))
                with act.Fori(0, NB) as b:
                    for g, x in enumerate(groups):
                        n = GP if x != "gn" else 1
                        act.wait_ge(T.sem, late(T, f"t{x}", b))
                        act.wait_ge(T.sem, late(T, f"s{groups[g - 2]}", b) if g >= 2
                                    else late(T, f"s{groups[-1]}", b - 1))
                        act.activation(kT[:, g % 2, 0, 0:n, :], t_ps[0][:, 0:n, :], ACT.Copy).then_inc(A.sem, 1)
                    act.wait_ge(V.sem, late(V, "sub", b))
                    act.activation(S[:, :, :], S[:, :, :], ACT.Exp, scale=scale).then_inc(A.sem, 1)

            @block.vector
            def _(dve):
                dve.wait_ge(init, 32)
                dve.wait_ge(mem0, 4)
                for r in range(4):
                    for h in range(2):
                        last = dve.tensor_copy(qd[32 * r:32 * r + 32, :, h, 4 * r:4 * r + 4],
                                               qT[32 * r:32 * r + 32, h, :].rearrange("p (b q) -> p b q", q=NQ))
                last.then_inc(V.sem, len(V.names))
                with dve.Fori(0, NB) as b:
                    for g, x in enumerate(groups):
                        n = GP if x != "gn" else 1
                        dve.wait_ge(T.sem, late(T, f"t{x}", b))
                        dve.wait_ge(T.sem, late(T, f"s{groups[g - 2]}", b) if g >= 2
                                    else late(T, f"s{groups[-1]}", b - 1))
                        dve.tensor_copy(kT[:, g % 2, 1, 0:n, :], t_ps[1][:, 0:n, :]).then_inc(V.sem, 1)
                        dve.wait_ge(T.sem, late(T, f"s{x}", b))
                        if g == 0:
                            dve.wait_ge(T.sem, late(T, "pv", b - 1))
                        dve.tensor_copy(S[:, g * GP:g * GP + n, :], s_ps[g % 2][:, 0:n, :]).then_inc(V.sem, 1)
                    dve.wait_ge(V.sem, late(V, "sgn", b))
                    dve.tensor_tensor(S[:, PAGES, :].rearrange("p (x q) -> p x q", q=NQ),
                                      S[:, PAGES, :].rearrange("p (x q) -> p x q", q=NQ), mid(new_mask[:, :], 8),
                                      ALU.add).then_inc(V.sem, 1)
                    dve.wait_ge(V.sem, late(V, "newmask", b))
                    dve.tensor_reduce(top[:, :], S[:, :, :].rearrange("p g x -> p x g"), AX.X, ALU.max)\
                       .then_inc(V.sem, 1)
                    dve.wait_ge(T.sem, late(T, "topT", b))
                    dve.tensor_reduce(topT[:, :], m_ps[0:32, 0:P], AX.X, ALU.max).then_inc(V.sem, 1)
                    dve.wait_ge(V.sem, late(V, "topT", b))
                    dve.tensor_scalar(diag[:, :], pr.ident[0:32, 0:32], topT[:, 0:1], None, ALU.mult).then_inc(V.sem, 1)
                    dve.wait_ge(T.sem, late(T, "topB", b))
                    dve.tensor_tensor(S[:, :, :], S[:, :, :], mid(b_ps[:, 0:32], NPG), ALU.subtract).then_inc(V.sem, 1)
                    dve.wait_ge(A.sem, late(A, "exp", b))
                    dve.tensor_reduce(sums[:, :], S[:, :, :].rearrange("p g x -> p x g"), AX.X, ALU.add)\
                       .then_inc(V.sem, 1)
                    dve.wait_ge(T.sem, late(T, "den", b))
                    dve.reciprocal(rden[:, :], m_ps[0:32, 256:257]).then_inc(V.sem, 1)
                    dve.wait_ge(V.sem, late(V, "rden", b))
                    dve.tensor_scalar(comb[:, :, 0:NQ], seqm.rearrange("r (h q) -> r h q", q=NQ), rden[:, 0:1], None, ALU.mult).then_inc(V.sem, 1)
                    dve.wait_ge(T.sem, late(T, "pv", b))
                    dve.wait_ge(V.sem, late(V, "comb", b))
                    dve.tensor_copy(O[:, :], o_ps[0:32, 0:W_B]).then_inc(V.sem, 1)
                    dve.wait_ge(T.sem, late(T, "fin", b))
                    dve.wait_ge(o_out, b * 16 + 16)
                    dve.tensor_copy(og[:, :], f_ps[0:NQ, 0:W_B]).then_inc(V.sem, 1)


def wait(eng, steps, name, t):
    eng.wait_ge(steps.sem, steps.at(name, t + 1))


def credit(eng, steps):
    (eng.engine_nop() if hasattr(eng, "engine_nop") else eng.nop()).then_inc(steps.sem, len(steps.names))


def half(h):
    return slice(HD * (h % 2), HD * (h % 2) + HD)


class Inverse:

    def __init__(self, st, n, levels, ident, masks):
        self.n, self.levels, self.ident, self.masks = n, levels, ident, masks
        self.X, self.XT = st.sb("X", [P, 6, n]), st.sb("XT", [P, 6, n])
        self.Y = st.sb("Y", [P, 6, n])
        self.AM = [st.sb(f"AM{b}", [P, 6, n]) for b in range(levels + 1)]
        lg = [(b, g) for b in range(1, levels + 1) for g in range(2)]
        self.pe_names = "x0 " + " ".join(f"Y{b}{g}" for b, g in lg) + " " + " ".join(f"W{b}{g}" for b, g in lg)
        self.pe_order = ["x0"]
        for b in range(1, levels + 1):
            self.pe_order += [f"Y{b}0", f"Y{b}1", f"W{b}0", f"W{b}1"]
        self.pe_names = " ".join(self.pe_order)
        self.act_names = "x0 " + " ".join(f"y{b}{g}" for b, g in lg)
        self.dve_names = "xt0 " + " ".join(f"x{b}{g}" for b, g in lg)
        self.pool_names = " ".join(f"am{b}" for b in range(levels + 1))

    def pool(self, eng, G, at, before):
        n = self.n
        before()
        for b in range(self.levels + 1):
            eng.tensor_tensor(self.AM[b][0:n, :, :], at, mid(self.masks[0:n, b, 0:n], 6), ALU.mult)\
               .then_inc(G.sem, 1)

    def pe(self, eng, T, A, V, G, t, banks, free):
        n = self.n
        v3 = lambda bank: bank[0:n, 0:3 * n].rearrange("p (h n) -> p h n", n=n)
        wait(eng, V, "xt0", t)
        free()
        for h in range(6):
            mm = eng.transpose(v3(banks[h // 3])[:, h % 3, :], self.XT[0:n, h, :], self.ident[0:n, 0:n])
        mm.then_inc(T.sem, 1)
        for b in range(1, self.levels + 1):
            wait(eng, G, f"am{b}", t)
            for g in range(2):
                if b == 1:
                    wait(eng, A, "x0", t)
                else:
                    wait(eng, V, f"x{b - 1}{g}", t)
                for j in range(3):
                    h = 3 * g + j
                    mm = eng.matmul(v3(banks[g])[:, j, :], self.AM[b][0:n, h, :], self.X[0:n, h, :],
                                    start=True, stop=True)
                mm.then_inc(T.sem, 1)
            for g in range(2):
                wait(eng, A, f"y{b}{g}", t)
                for j in range(3):
                    h = 3 * g + j
                    if b < self.levels:
                        eng.matmul(v3(banks[2 + g])[:, j, :], self.XT[0:n, h, :], self.Y[0:n, h, :],
                                   start=True, stop=True)
                    mm = eng.matmul(v3(banks[4 + g])[:, j, :], self.Y[0:n, h, :], self.XT[0:n, h, :],
                                    start=True, stop=True)
                mm.then_inc(T.sem, 1)

    def act(self, eng, T, A, t, banks):
        n = self.n
        v3 = lambda bank: bank[0:n, 0:3 * n].rearrange("p (h n) -> p h n", n=n)
        wait(eng, T, "x0", t)
        for g in range(2):
            last = eng.activation(self.X[0:n, 3 * g:3 * g + 3, :], v3(banks[g]), ACT.Copy)
        last.then_inc(A.sem, 1)
        for b in range(1, self.levels + 1):
            for g in range(2):
                wait(eng, T, f"Y{b}{g}", t)
                eng.activation(self.Y[0:n, 3 * g:3 * g + 3, :], v3(banks[g]), ACT.Copy).then_inc(A.sem, 1)

    def dve_first(self, eng, V, G, t):
        n = self.n
        wait(eng, G, "am0", t)
        eng.tensor_tensor(self.XT[0:n, :, :], mid(self.ident[0:n, 0:n], 6), self.AM[0][0:n, :, :], ALU.subtract)\
           .then_inc(V.sem, 1)

    def dve(self, eng, T, V, t, banks):
        n = self.n
        v3 = lambda bank: bank[0:n, 0:3 * n].rearrange("p (h n) -> p h n", n=n)
        for b in range(1, self.levels + 1):
            for g in range(2):
                wait(eng, T, f"W{b}{g}", t)
                hs = slice(3 * g, 3 * g + 3)
                if b < self.levels:
                    eng.tensor_tensor(self.X[0:n, hs, :], self.X[0:n, hs, :], v3(banks[2 + g]), ALU.subtract)
                eng.tensor_tensor(self.XT[0:n, hs, :], self.XT[0:n, hs, :], v3(banks[4 + g]), ALU.subtract)\
                   .then_inc(V.sem, 1)


def load_ahead(sp, sample, load, store):
    load(0)
    if not sample:
        with sp.Fori(1, TILES) as t:
            load(t)
            store(t - 1)
    store(0 if sample else TILES - 1)


def over_tiles(eng, sample, body):
    if sample:
        body(0)
    else:
        with eng.Fori(0, TILES) as t:
            body(t)


XS = range(12)
HEADS_OF_BANK = ((0, 2), (1, 3), (4,), (5,))
BANK_OF_HEAD = {h: (j, m) for j, hs in enumerate(HEADS_OF_BANK) for m, h in enumerate(hs)}
VX_ORDER = "vx0 vx1 us0 vx2 us1 vx3 us2 vx4 us3 vx5 us4 us5"


def gdn(nc, pr, S, sample, consts):
    n = NS if sample else P
    base = SEQ if sample else 0
    seg, strict, incl, levels, seq, neg_a, dt, norm_g = consts
    with Stage(nc) as st:
        cq, cz, cb = st.sb("cq", [P, 9, n]), st.sb("cz", [P, 3, n]), st.sb("cb", [12, n])
        sq = st.sb("sq", [P, 2, W_A])
        ss = st.sb("ss", [P, 12])
        bl = st.sb("bl", [P, 12])
        qn, kn, v, z = (st.sb(x, [P, 6, HD]) for x in ("qn", "kn", "v", "z"))
        kb, kd, vb = (st.sb(x, [P, 6, HD]) for x in ("kb", "kd", "vb"))
        eb, y, ny, ey, sp, g, beta, beg = (st.sb(x, [P, 6]) for x in ("eb", "y", "ny", "ey", "sp", "g", "beta", "beg"))
        gB = st.sb("gB", [P, 6, P])
        gs = st.sb("gs", [P, 2, 8])
        egam, egd, egl = (st.sb(x, [P, 6]) for x in ("egam", "egd", "egl"))
        glp = st.sb("glp", [P, 3])
        E = st.sb("E", [P, 6, n])
        E2 = st.sb("E2", [P, 6, 2, n])
        kT = st.sb("kT", [P, 3, n])
        kq = st.sb("kq", [P, 3, 2, n])
        AP_ = st.sb("AP", [P, 6, 2, n])
        rhs, vn, o, osq = (st.sb(x, [P, 6, HD]) for x in ("rhs", "vn", "o", "osq"))
        oss = st.sb("oss", [P, 6])
        res = st.sb("res", [P, 6, HD])
        if sample:
            xm = st.sb("xm", [NS, NB, HD])
            ks, qs = st.sb("ks", [NS, 6, HD]), st.sb("qs", [NS, 6, HD])
            vx = st.sb("vx", [NS, 2, NB, HD])
            egb = st.sb("egb", [P, 6, NB])
        B = [st.ps(f"b{j}", [P, 512]) for j in range(8)]
        inv = Inverse(st, n, 1 if sample else 6, pr.ident, levels)
        loaded, stored = st.sem("loaded"), st.sem("stored")
        xs_pe = " ".join(f"X{i}" for i in XS) if sample else "KS"
        us_pe = " ".join(f"U{i}" for i in range(6)) if sample else "dS"
        T = st.steps("pe_steps", f"flip gam gamb back A0 A1 A2 A3 {inv.pe_names} {xs_pe} VN O2 "
                     + ("egb " if sample else "") + us_pe)
        A = st.steps("act_steps", "sqq sqk v z eb ln rs ey l1 E eg egd egl kT kbT " + inv.act_names
                     + " vn" + (" egb" if sample else "") + " oln ors")
        V = st.steps("dve_steps", "bl y ny eb1 beta ss sp g gbc gams gd dif qn kn kb kd vb beg qT ap0 ap1 ap2 ap3 "
                     + inv.dve_names + " "
                     + (" ".join(f"xm{i} xr{i}" for i in XS) if sample else "")
                     + " r1 rhs qs o glp sd "
                     + (VX_ORDER if sample else "us")
                     + " osq oss on og oz")
        G = st.steps("pool_steps", "es ei " + inv.pool_names)
        f3 = lambda ap: ap.rearrange("p h d -> p (h d)")
        nat = lambda bank: bank[0:n, 0:W_A].rearrange("p (h d) -> p h d", d=HD)
        par = lambda hh, j: B[6 + hh][0:n, j * 3 * HD:(j + 1) * 3 * HD].rearrange("p (c d) -> p c d", d=HD)
        chan = lambda bank: bank[:, 0:3 * n].rearrange("p (c n) -> p c n", n=n)
        cols3 = pr.cols.rearrange("f p n -> p f n")
        with nc.Block() as block:
            @block.sync
            def _(sp_):
                sp_.nop().then_inc(stored, 16)

                def load(t):
                    wait(sp_, T, "flip", t - 1)
                    where = bass.ds(t * P + base, n)
                    sp_.dma_start(cq[:, :, :], cols3[:, B_QKV:B_QKV + 9, where]).then_inc(loaded, 16)
                    sp_.dma_start(cz[:, :, :], cols3[:, B_Z:B_Z + 3, where]).then_inc(loaded, 16)
                    sp_.dma_start(cb[:, :], pr.cols[B_BETA, 0:12, where]).then_inc(loaded, 16)

                def store(t):
                    wait(sp_, V, "oz", t)
                    sp_.dma_start(pr.o_raw[bass.ds(t * P + base, n), 0:W_A], f3(res[0:n, :, :])).then_inc(stored, 16)
                load_ahead(sp_, sample, load, store)
                sp_.wait_ge(stored, 16 * (2 if sample else TILES + 1))

            @block.gpsimd
            def _(pool):
                credit(pool, G)

                def body(t):
                    wait(pool, A, "E", t)
                    wait(pool, V, "ap3", t - 1)
                    pool.tensor_tensor(E2[0:n, :, 0, :], E[0:n, :, :], mid(strict[0:n, 0:n], 6), ALU.mult)\
                        .then_inc(G.sem, 1)
                    pool.tensor_tensor(E2[0:n, :, 1, :], E[0:n, :, :], mid(incl[0:n, 0:n], 6), ALU.mult)\
                        .then_inc(G.sem, 1)
                    inv.pool(pool, G, AP_[0:n, :, 0, :], lambda: wait(pool, V, "ap3", t))
                over_tiles(pool, sample, body)

            @block.tensor
            def _(pe):
                credit(pe, T)

                def body(t):
                    pe.wait_ge(loaded, t * 48 + 48)
                    wait(pe, V, "us" if not sample else "us5", t - 1)
                    wait(pe, V, "o", t - 1)
                    for c in range(9):
                        pe.transpose(B[c // 3][0:n, (c % 3) * P:(c % 3 + 1) * P], cq[:, c, :], pr.ident[:, :])
                    for c in range(3):
                        pe.transpose(B[3][0:n, c * P:(c + 1) * P], cz[:, c, :], pr.ident[:, :])
                    pe.transpose(B[7][0:n, 0:12], cb[:, :], pr.ident[0:12, 0:12]).then_inc(T.sem, 1)
                    wait(pe, V, "g", t)
                    pe.matmul(B[4][0:n, 0:6], incl[0:n, 0:n], g[0:n, :], start=True, stop=True)
                    pe.matmul(B[4][0:n, 8:14], seg[0:n, 0:n], g[0:n, :], start=True, stop=True).then_inc(T.sem, 1)
                    wait(pe, V, "gbc", t)
                    for h in range(6):
                        mm = pe.matmul(B[5 + h // 3][0:n, (h % 3) * n:(h % 3 + 1) * n], gB[0:n, h, 0:n],
                                       incl[0:n, 0:n], start=True, stop=True)
                    mm.then_inc(T.sem, 1)
                    wait(pe, V, "kb", t)
                    wait(pe, A, "v", t)
                    for j, src in enumerate((kn, kb, qn)):
                        for c in range(3):
                            mm = pe.transpose(chan(B[j])[:, c, :], f3(src[0:n, :, :])[:, c * P:(c + 1) * P],
                                              pr.ident[0:n, 0:n])
                    mm.then_inc(T.sem, 1)
                    wait(pe, V, "qT", t)
                    wait(pe, A, "kbT", t)
                    wait(pe, V, "dif", t)
                    wait(pe, A, "z", t)
                    for h in range(6):
                        j, m = BANK_OF_HEAD[h]
                        mm = pe.matmul(B[3 + j][0:n, m * 2 * n:(m + 1) * 2 * n],
                                       kT[half(h), h // 2, :], kq[half(h), h // 2, :, :].rearrange("p a n -> p (a n)"),
                                       start=True, stop=True)
                        if h == HEADS_OF_BANK[j][-1]:
                            mm.then_inc(T.sem, 1)
                    inv.pe(pe, T, A, V, G, t, B, lambda: None)
                    if sample:
                        for i in XS:
                            h = i % 6
                            if i >= 2:
                                wait(pe, V, f"xm{i - 2}", t)
                            src = kT[half(h), h // 2, :] if i < 6 else kq[half(h), h // 2, 1, :]
                            pe.matmul(B[6 + i % 2][0:n, :], src, S[half(h), :, h // 2, :],
                                      start=True, stop=True).then_inc(T.sem, 1)
                    else:
                        wait(pe, V, "us", t - 1)
                        for j in range(2):
                            for h in range(6):
                                src = kT[half(h), h // 2, :] if j == 0 else kq[half(h), h // 2, 1, :]
                                mm = pe.matmul(par(h % 2, j)[:, h // 2, :], src, S[half(h), h // 2, :],
                                               start=True, stop=True)
                        mm.then_inc(T.sem, 1)
                    wait(pe, V, "rhs", t)
                    for h in range(6):
                        mm = pe.matmul(nat(B[0])[:, h, :], inv.XT[0:n, h, :], rhs[0:n, h, :], start=True, stop=True)
                    mm.then_inc(T.sem, 1)
                    wait(pe, A, "vn", t)
                    for h in range(6):
                        mm = pe.matmul(nat(B[1])[:, h, :], AP_[0:n, h, 1, :], vn[0:n, h, :], start=True, stop=True)
                    mm.then_inc(T.sem, 1)
                    if sample:
                        for h in range(6):
                            mm = pe.matmul(B[4][:, h * NB:(h + 1) * NB], gB[0:n, h, :], seq[0:n, :], start=True, stop=True)
                        mm.then_inc(T.sem, 1)
                        for h in range(6):
                            if h >= 2:
                                wait(pe, V, f"us{h - 2}", t)
                            wait(pe, V, f"vx{h}", t)
                            pe.matmul(B[2 + h % 2][:, :], f3(kd[0:n, :, :])[:, (h // 2) * P:(h // 2 + 1) * P],
                                      vx[:, h % 2, :, :].rearrange("p b d -> p (b d)"), start=True, stop=True)\
                              .then_inc(T.sem, 1)
                    else:
                        for p in range(3):
                            mm = pe.matmul(B[2][:, p * P:(p + 1) * P], f3(kd[0:n, :, :])[:, p * P:(p + 1) * P],
                                           f3(vn[0:n, :, :])[:, p * P:(p + 1) * P], start=True, stop=True)
                        mm.then_inc(T.sem, 1)
                over_tiles(pe, sample, body)

            @block.scalar
            def _(act):
                credit(act, A)

                def body(t):
                    wait(act, T, "flip", t)
                    wait(act, V, "ss", t - 1)
                    act.activation(sq[0:n, 0, :], B[0][0:n, 0:W_A], ACT.Square).then_inc(A.sem, 1)
                    act.activation(sq[0:n, 1, :], B[1][0:n, 0:W_A], ACT.Square).then_inc(A.sem, 1)
                    wait(act, V, "vb", t - 1)
                    act.activation(f3(v[0:n, :, :]), B[2][0:n, 0:W_A], ACT.Copy).then_inc(A.sem, 1)
                    wait(act, V, "oz", t - 1)
                    act.activation(f3(z[0:n, :, :]), B[3][0:n, 0:W_A], ACT.Copy).then_inc(A.sem, 1)
                    wait(act, V, "bl", t)
                    act.activation(eb[0:n, :], bl[0:n, 0:6], ACT.Exp, scale=-1.0).then_inc(A.sem, 1)
                    wait(act, V, "ss", t)
                    act.activation(ss[0:n, :], ss[0:n, :], ACT.Ln, bias=pr.eps[0:n, :]).then_inc(A.sem, 1)
                    wait(act, A, "ln", t)
                    act.activation(ss[0:n, :], ss[0:n, :], ACT.Exp, scale=-0.5).then_inc(A.sem, 1)
                    wait(act, V, "ny", t)
                    act.activation(ey[0:n, :], ny[0:n, :], ACT.Exp).then_inc(A.sem, 1)
                    wait(act, A, "ey", t)
                    act.activation(ey[0:n, :], ey[0:n, :], ACT.Ln, bias=pr.ones[0:n, 0:1]).then_inc(A.sem, 1)
                    wait(act, V, "dif", t)
                    act.activation(E[0:n, :, :], E[0:n, :, :], ACT.Exp).then_inc(A.sem, 1)
                    wait(act, V, "gd", t)
                    act.activation(egam[0:n, :], gs[0:n, 0, 0:6], ACT.Exp).then_inc(A.sem, 1)
                    act.activation(egd[0:n, :], egd[0:n, :], ACT.Exp).then_inc(A.sem, 1)
                    act.activation(egl[0:n, :], gs[0:n, 1, 0:6], ACT.Exp).then_inc(A.sem, 1)
                    wait(act, T, "back", t)
                    act.activation(kT[:, :, :], chan(B[0]), ACT.Copy).then_inc(A.sem, 1)
                    act.activation(kq[:, :, 0, :], chan(B[1]), ACT.Copy).then_inc(A.sem, 1)
                    inv.act(act, T, A, t, B)
                    wait(act, T, "VN", t)
                    act.activation(f3(vn[0:n, :, :]), B[0][0:n, 0:W_A], ACT.Copy).then_inc(A.sem, 1)
                    if sample:
                        wait(act, T, "egb", t)
                        act.activation(egb[:, :, :].rearrange("p h b -> p (h b)"), B[4][:, 0:6 * NB], ACT.Exp)\
                           .then_inc(A.sem, 1)
                    wait(act, V, "oss", t)
                    act.activation(oss[0:n, :], oss[0:n, :], ACT.Ln, scale=1.0 / HD, bias=pr.eps[0:n, :])\
                       .then_inc(A.sem, 1)
                    wait(act, A, "oln", t)
                    act.activation(oss[0:n, :], oss[0:n, :], ACT.Exp, scale=-0.5).then_inc(A.sem, 1)
                over_tiles(act, sample, body)

            @block.vector
            def _(dve):
                credit(dve, V)

                def body(t):
                    def tt(out, a, b, op):
                        dve.tensor_tensor(out, a, b, op).then_inc(V.sem, 1)
                    wait(dve, T, "flip", t)
                    wait(dve, A, "eb", t - 1)
                    dve.tensor_copy(bl[0:n, :], B[7][0:n, 0:12]).then_inc(V.sem, 1)
                    wait(dve, V, "bl", t)
                    tt(y[0:n, :], bl[0:n, 6:12], dt[0:n, :], ALU.add)
                    wait(dve, V, "y", t)
                    dve.scalar_tensor_tensor(ny[0:n, :], y[0:n, :], -1.0, y[0:n, :], ALU.mult, ALU.min)\
                       .then_inc(V.sem, 1)
                    wait(dve, A, "eb", t)
                    dve.tensor_scalar(beta[0:n, :], eb[0:n, :], 1.0, None, ALU.add).then_inc(V.sem, 1)
                    wait(dve, V, "eb1", t)
                    dve.reciprocal(beta[0:n, :], beta[0:n, :]).then_inc(V.sem, 1)
                    wait(dve, A, "sqk", t)
                    dve.tensor_reduce(ss[0:n, :], sq[0:n, :, :].rearrange("p a (h d) -> p (a h) d", d=HD), AX.X,
                                      ALU.add).then_inc(V.sem, 1)
                    wait(dve, A, "l1", t)
                    dve.scalar_tensor_tensor(sp[0:n, :], y[0:n, :], 0.0, ey[0:n, :], ALU.max, ALU.add)\
                       .then_inc(V.sem, 1)
                    wait(dve, V, "sp", t)
                    tt(g[0:n, :], sp[0:n, :], neg_a[0:n, :], ALU.mult)
                    wait(dve, V, "g", t)
                    dve.tensor_copy(gB[0:n, :, :], bc(g[0:n, :], P)).then_inc(V.sem, 1)
                    wait(dve, T, "gam", t)
                    dve.tensor_copy(gs[0:n, :, 0:6], B[4][0:n, 0:16].rearrange("p (a b) -> p a b", b=8)[:, :, 0:6])\
                       .then_inc(V.sem, 1)
                    wait(dve, V, "gams", t)
                    tt(egd[0:n, :], gs[0:n, 1, 0:6], gs[0:n, 0, 0:6], ALU.subtract)
                    wait(dve, T, "gamb", t)
                    wait(dve, G, "ei", t - 1)
                    for h in range(6):
                        last = dve.tensor_scalar(E[0:n, h, :], B[5 + h // 3][0:n, (h % 3) * n:(h % 3 + 1) * n],
                                                 gs[0:n, 0, h:h + 1], 0.0, ALU.subtract, ALU.min)
                    last.then_inc(V.sem, 1)
                    wait(dve, A, "rs", t)
                    dve.scalar_tensor_tensor(qn[0:n, :, :], nat(B[0]), float(HD) ** -0.5, bc(ss[0:n, 0:6], HD),
                                             ALU.mult, ALU.mult).then_inc(V.sem, 1)
                    tt(kn[0:n, :, :], nat(B[1]), bc(ss[0:n, 6:12], HD), ALU.mult)
                    wait(dve, V, "kn", t)
                    tt(kb[0:n, :, :], kn[0:n, :, :], bc(beta[0:n, :], HD), ALU.mult)
                    wait(dve, A, "egl", t)
                    tt(kd[0:n, :, :], kn[0:n, :, :], bc(egd[0:n, :], HD), ALU.mult)
                    tt(vb[0:n, :, :], v[0:n, :, :], bc(beta[0:n, :], HD), ALU.mult)
                    tt(beg[0:n, :], beta[0:n, :], egam[0:n, :], ALU.mult)
                    wait(dve, T, "back", t)
                    dve.tensor_copy(kq[:, :, 1, :], chan(B[2])).then_inc(V.sem, 1)
                    wait(dve, G, "ei", t)
                    for j, hs in enumerate(HEADS_OF_BANK):
                        wait(dve, T, f"A{j}", t)
                        hs = slice(hs[0], hs[-1] + 1, 2)
                        two = lambda x: x[0:n, hs, :, :].rearrange("p h a n -> p h (a n)")
                        nh = 2 if j < 2 else 1
                        tt(two(AP_), B[3 + j][0:n, 0:nh * 2 * n].rearrange("p (h x) -> p h x", h=nh), two(E2), ALU.mult)
                    inv.dve_first(dve, V, G, t)
                    inv.dve(dve, T, V, t, B)
                    if sample:
                        for i in XS:
                            wait(dve, T, f"X{i}", t)
                            if i:
                                wait(dve, V, f"xr{i - 1}", t)
                            tt(xm[:, :, :], B[6 + i % 2][0:n, :].rearrange("p (b d) -> p b d", d=HD),
                               bc(seq[0:n, :], HD), ALU.mult)
                            wait(dve, V, f"xm{i}", t)
                            dve.tensor_reduce((ks, qs)[i // 6][:, i % 6, :], xm[:, :, :].rearrange("p b d -> p d b"),
                                              AX.X, ALU.add).then_inc(V.sem, 1)
                        wait(dve, V, "xr11", t)
                        KS, QS = [(x[:, 0::2, :], x[:, 1::2, :]) for x in (ks, qs)]
                    else:
                        wait(dve, T, "KS", t)
                        KS, QS = [(par(0, j), par(1, j)) for j in range(2)]
                    wait(dve, V, "beg", t)
                    for hh in range(2):
                        last = dve.tensor_tensor(rhs[0:n, hh::2, :], KS[hh], bc(beg[0:n, hh::2], HD), ALU.mult)
                    last.then_inc(V.sem, 1)
                    wait(dve, V, "r1", t)
                    tt(rhs[0:n, :, :], vb[0:n, :, :], rhs[0:n, :, :], ALU.subtract)
                    for hh in range(2):
                        last = dve.tensor_tensor(o[0:n, hh::2, :], QS[hh], bc(egam[0:n, hh::2], HD), ALU.mult)
                    last.then_inc(V.sem, 1)
                    wait(dve, T, "O2", t)
                    wait(dve, V, "qs", t)
                    tt(o[0:n, :, :], o[0:n, :, :], nat(B[1]), ALU.add)
                    if sample:
                        dve.engine_nop().then_inc(V.sem, 1)
                        wait(dve, A, "egb", t)
                        for hh in range(2):
                            for p in range(3):
                                last = dve.tensor_tensor(S[half(hh), :, p, :], S[half(hh), :, p, :],
                                                         bc(egb[half(hh), 2 * p + hh, :], HD), ALU.mult)
                        last.then_inc(V.sem, 1)
                    else:
                        dve.tensor_copy(glp[0:HD, :], egl[0:HD, 0:6:2])
                        dve.tensor_copy(glp[HD:P, :], egl[HD:P, 1:6:2]).then_inc(V.sem, 1)
                        wait(dve, V, "glp", t)
                        tt(S[:, :, :], S[:, :, :], bc(glp[:, :], HD), ALU.mult)
                        wait(dve, T, "dS", t)
                        wait(dve, V, "sd", t)
                        for hh in range(2):
                            last = dve.tensor_tensor(
                                S[half(hh), :, :], S[half(hh), :, :],
                                B[2][half(hh), 0:W_A].rearrange("p (c d) -> p c d", d=P)[:, :, HD * hh:HD * hh + HD],
                                ALU.add)
                        last.then_inc(V.sem, 1)
                    if sample:
                        sample_updates(t)
                    wait(dve, V, "o", t)
                    tt(osq[0:n, :, :], o[0:n, :, :], o[0:n, :, :], ALU.mult)
                    wait(dve, V, "osq", t)
                    dve.tensor_reduce(oss[0:n, :], osq[0:n, :, :], AX.X, ALU.add).then_inc(V.sem, 1)
                    wait(dve, A, "ors", t)
                    tt(o[0:n, :, :], o[0:n, :, :], bc(oss[0:n, :], HD), ALU.mult)
                    wait(dve, V, "on", t)
                    tt(o[0:n, :, :], o[0:n, :, :], mid(norm_g[0:n, :], 6), ALU.mult)
                    wait(dve, V, "og", t)
                    wait(dve, A, "z", t)
                    if not sample:
                        dve.wait_ge(stored, t * 16 + 16)
                    tt(res[0:n, :, :], o[0:n, :, :], z[0:n, :, :], ALU.mult)

                def sample_updates(t):
                    for h in range(6):
                        if h >= 2:
                            wait(dve, T, f"U{h - 2}", t)
                        wait(dve, A, "vn", t)
                        dve.tensor_tensor(vx[:, h % 2, :, :], mid(vn[0:n, h, :], NB), bc(seq[0:n, :], HD), ALU.mult)\
                           .then_inc(V.sem, 1)
                        if h >= 1:
                            wait(dve, T, f"U{h - 1}", t)
                            add_state(t, h - 1)
                    wait(dve, T, "U5", t)
                    add_state(t, 5)

                def add_state(t, h):
                    wait(dve, V, "sd", t)
                    dve.tensor_tensor(S[half(h), :, h // 2, :], S[half(h), :, h // 2, :],
                                      B[2 + h % 2][half(h), :].rearrange("p (b d) -> p b d", d=HD), ALU.add)\
                       .then_inc(V.sem, 1)
                over_tiles(dve, sample, body)


def rwkv(nc, pr, S, sample, consts):
    n = NS if sample else P
    base = SEQ if sample else 0
    (mask2, levels, seq, scan, ones_half, w2a2, g2, nw0, na0, k_k, k_a, r_k, lnw, lnb, eps12, eps_gn) = consts
    DEC = math.exp(-0.5)
    with Stage(nc) as st:
        c = st.sb("c", [P, 11, n])
        th, sg = st.sb("th", [64, n]), st.sb("sg", [P, n])
        sig = st.sb("sig", [P, 2, 3, n])
        G_ = st.sb("G", [P, 3, n])
        Dx = st.sb("Dx", [P, 3, n])
        ep, em, ex = (st.sb(x, [P, 3, n]) for x in ("ep", "em", "ex"))
        eg, gm = st.sb("eg", [P, 3]), st.sb("gm", [P, 3])
        kx, kk, ksq, rs = (st.sb(x, [P, 3, n]) for x in ("kx", "kk", "ksq", "rs"))
        kp, kt_, bo = (st.sb(x, [P, 3, n]) for x in ("kp", "kt", "bo"))
        KR = st.sb("KR", [P, 3, 2, n])
        Bt, Kt = st.sb("Bt", [P, 3, n]), st.sb("Kt", [P, 3, n])
        v, bn, kn, gate = (st.sb(x, [P, 6, HD]) for x in ("v", "bn", "kn", "gate"))
        bs = st.sb("bs", [P, 6])
        tick = st.sb("tick", [1, 8])
        APb, APk = st.sb("APb", [P, 6, 2, n]), st.sb("APk", [P, 6, 2, n])
        Sh = st.sb("Sh", [P, 3, HD]) if not sample else S
        rhs, sa, o, osq = (st.sb(x, [P, 6, HD]) for x in ("rhs", "sa", "o", "osq"))
        om, ov = st.sb("om", [P, 6]), st.sb("ov", [P, 6])
        res = st.sb("res", [P, 6, HD])
        if sample:
            xm = st.sb("xm", [NS, NB, HD])
            ks, qs = st.sb("ks", [NS, 6, HD]), st.sb("qs", [NS, 6, HD])
            vx = st.sb("vx", [NS, 2, 2, NB, HD])
        B = [st.ps(f"b{j}", [P, 512]) for j in range(8)]
        inv = Inverse(st, n, 1 if sample else 6, pr.ident, levels)
        loaded, stored, cleared = st.sem("loaded"), st.sem("stored"), st.sem("cleared")
        T = st.steps("pe_steps", "wy ay gy kss bs flip b0 b1 b2 b3 k0 k1 k2 k3 " + inv.pe_names
                     + (" " + " ".join(f"X{i}" for i in XS) if sample else "") + " RH SA O "
                     + (" ".join(f"U{i}" for i in range(6)) if sample else "dS"))
        A = st.steps("act_steps", "e1 e2 ew ea gate ep em ex eg kln krs v bn kn " + inv.act_names + " rhs sa oln ors")
        V = st.steps("dve_steps", "th1 th2 th3 sg1 sg2 kx ksq s1 s2 scan gm D Dx kk kp1 kp2 bo1 bo2 K R B1 B K2 bs "
                     "ab0 ab1 ab2 ab3 ak0 ak1 ak2 ak3 " + inv.dve_names + " "
                     + (" ".join(f"xm{i} xr{i}" for i in XS) + " r0" if sample else "Sh") + " o1 "
                     + (VX_ORDER + " us" if sample else "us1 us")
                     + " om omn oc osq ov on ow ob bv obv og")
        Gp = st.steps("pool_steps", inv.pool_names)
        f3 = lambda ap: ap.rearrange("p h d -> p (h d)")
        nat = lambda bank: bank[0:n, 0:W_A].rearrange("p (h d) -> p h d", d=HD)
        par = lambda b, hh: B[b + hh][0:n, 0:3 * HD].rearrange("p (c d) -> p c d", d=HD)
        chan = lambda bank: bank[:, 0:3 * n].rearrange("p (c n) -> p c n", n=n)
        cols3 = pr.cols.rearrange("f p n -> p f n")
        with nc.Block() as block:
            @block.sync
            def _(sp):
                sp.nop().then_inc(stored, 16)

                def load(t):
                    wait(sp, T, "flip", t - 1)
                    wait(sp, V, "R", t - 1)
                    sp.dma_start(c[:, :, :], cols3[:, B_RWKV:B_RWKV + 11, bass.ds(t * P + base, n)])\
                      .then_inc(loaded, 16)

                def store(t):
                    wait(sp, V, "og", t)
                    sp.dma_start(pr.o_raw[bass.ds(t * P + base, n), W_A + W_B:D], f3(res[0:n, :, :]))\
                      .then_inc(stored, 16)
                load_ahead(sp, sample, load, store)
                sp.wait_ge(stored, 16 * (2 if sample else TILES + 1))

            @block.gpsimd
            def _(pool):
                pool.memset(APb[:, :, :, :], 0.0).then_inc(cleared, 1)
                pool.memset(APk[:, :, :, :], 0.0).then_inc(cleared, 1)
                credit(pool, Gp)

                def body(t):
                    inv.pool(pool, Gp, APb[0:n, :, 0, :], lambda: wait(pool, V, "ab3", t))
                over_tiles(pool, sample, body)

            @block.tensor
            def _(pe):
                credit(pe, T)

                def body(t):
                    pe.wait_ge(loaded, t * 16 + 16)
                    wait(pe, V, "us", t - 1)
                    wait(pe, V, "o1", t - 1)
                    wait(pe, V, "th3", t)
                    for j in range(3):
                        mm = pe.matmul(chan(B[0])[:, j, :], w2a2[0:64, j * P:(j + 1) * P], th[:, :], start=True, stop=True)
                    mm.then_inc(T.sem, 1)
                    for j in range(3):
                        mm = pe.matmul(chan(B[1])[:, j, :], w2a2[64:P, j * P:(j + 1) * P], c[64:P, 9, :],
                                       start=True, stop=True)
                    mm.then_inc(T.sem, 1)
                    wait(pe, V, "sg2", t)
                    pe.matmul(B[2][0:n, 0:W_C], sg[:, :], g2[:, :], start=True, stop=True).then_inc(T.sem, 1)
                    wait(pe, V, "ksq", t)
                    pe.matmul(B[3][:, 0:3 * n], ones_half[:, :], ksq[:, :, :].rearrange("p c n -> p (c n)"),
                              start=True, stop=True).then_inc(T.sem, 1)
                    wait(pe, V, "bo2", t)
                    for j in range(3):
                        mm = pe.matmul(B[4][0:n, 2 * j:2 * j + 2], bo[:, j, :], ones_half[:, 0:P:HD],
                                       start=True, stop=True)
                    mm.then_inc(T.sem, 1)
                    wait(pe, V, "K2", t)
                    for b, src in ((5, None), (6, Bt), (7, Kt)):
                        for j in range(3):
                            s = c[:, 6 + j, :] if src is None else src[:, j, :]
                            mm = pe.transpose(B[b][0:n, j * P:(j + 1) * P], s, pr.ident[:, :])
                    mm.then_inc(T.sem, 1)
                    wait(pe, A, "krs", t)
                    wait(pe, A, "v", t)
                    wait(pe, V, "bs", t)
                    wait(pe, A, "kn", t)
                    for name, left, b0 in (("b", Bt, 0), ("k", Kt, 4)):
                        for h in range(6):
                            j, m = BANK_OF_HEAD[h]
                            mm = pe.matmul(B[b0 + j][0:n, m * 2 * n:(m + 1) * 2 * n], left[half(h), h // 2, :],
                                           KR[half(h), h // 2, :, :].rearrange("p a n -> p (a n)"), start=True, stop=True)
                            if h == HEADS_OF_BANK[j][-1]:
                                mm.then_inc(T.sem, 1)

                    def free():
                        wait(pe, V, "ak3", t)
                        wait(pe, A, "kn", t)
                    inv.pe(pe, T, A, V, Gp, t, B, free)
                    if sample:
                        for i in XS:
                            h = i % 6
                            if i >= 2:
                                wait(pe, V, f"xm{i - 2}", t)
                            pe.matmul(B[6 + i % 2][0:n, :], KR[half(h), h // 2, i // 6, :], S[half(h), :, h // 2, :],
                                      start=True, stop=True).then_inc(T.sem, 1)
                        wait(pe, V, "xm11", t)
                    else:
                        wait(pe, V, "Sh", t)
                    for h in range(6):
                        if not sample:
                            pe.matmul(par(6, h % 2)[:, h // 2, :], KR[half(h), h // 2, 0, :], Sh[half(h), h // 2, :],
                                      start=True, stop=False)
                        mm = pe.matmul(par(6, h % 2)[:, h // 2, :], APk[0:n, h, 0, :], v[0:n, h, :], start=sample, stop=True)
                    mm.then_inc(T.sem, 1)
                    wait(pe, A, "rhs", t)
                    for h in range(6):
                        mm = pe.matmul(nat(B[0])[:, h, :], inv.XT[0:n, h, :], rhs[0:n, h, :], start=True, stop=True)
                    mm.then_inc(T.sem, 1)
                    wait(pe, A, "sa", t)
                    for h in range(6):
                        if not sample:
                            pe.matmul(par(4, h % 2)[:, h // 2, :], KR[half(h), h // 2, 1, :], Sh[half(h), h // 2, :],
                                      start=True, stop=False)
                        pe.matmul(par(4, h % 2)[:, h // 2, :], APk[0:n, h, 1, :], v[0:n, h, :], start=sample, stop=False)
                        mm = pe.matmul(par(4, h % 2)[:, h // 2, :], APb[0:n, h, 1, :], sa[0:n, h, :], start=False, stop=True)
                    mm.then_inc(T.sem, 1)
                    if sample:
                        for h in range(6):
                            if h >= 2:
                                wait(pe, V, f"us{h - 2}", t)
                            wait(pe, V, f"vx{h}", t)
                            for j, left in enumerate((bn, kn)):
                                mm = pe.matmul(B[2 + h % 2][:, :], f3(left[0:n, :, :])[:, (h // 2) * P:(h // 2 + 1) * P],
                                               vx[:, h % 2, j, :, :].rearrange("p b d -> p (b d)"),
                                               start=(j == 0), stop=(j == 1))
                            mm.then_inc(T.sem, 1)
                    else:
                        for p in range(3):
                            pair = slice(p * P, (p + 1) * P)
                            pe.matmul(B[2][:, pair], f3(bn[0:n, :, :])[:, pair], f3(sa[0:n, :, :])[:, pair],
                                      start=True, stop=False)
                            mm = pe.matmul(B[2][:, pair], f3(kn[0:n, :, :])[:, pair], f3(v[0:n, :, :])[:, pair],
                                           start=False, stop=True)
                        mm.then_inc(T.sem, 1)
                over_tiles(pe, sample, body)

            @block.scalar
            def _(act):
                credit(act, A)

                def body(t):
                    def go(*a, **k):
                        act.activation(*a, **k).then_inc(A.sem, 1)
                    act.wait_ge(loaded, t * 16 + 16)
                    wait(act, T, "gy", t - 1)
                    go(th[:, :], c[0:64, 9, :], ACT.Exp, scale=-2.0)
                    go(sg[:, :], c[:, 10, :], ACT.Exp, scale=-1.0)
                    for j, (name, bank, bias) in enumerate((("wy", B[0], nw0), ("ay", B[1], na0))):
                        wait(act, T, name, t)
                        wait(act, V, "Dx" if j == 0 else "B", t - 1)
                        for m in range(3):
                            last = act.activation(sig[:, j, m, :], chan(bank)[:, m, :], ACT.Exp, scale=-1.0,
                                                  bias=bias[:, m:m + 1])
                        last.then_inc(A.sem, 1)
                    wait(act, T, "gy", t)
                    wait(act, V, "og", t - 1)
                    go(f3(gate[0:n, :, :]), B[2][0:n, 0:W_C], ACT.Copy)
                    wait(act, V, "Dx", t)
                    go(ep[:, :, :], G_[:, :, :], ACT.Exp, scale=DEC)
                    go(em[:, :, :], G_[:, :, :], ACT.Exp, scale=-DEC)
                    go(ex[:, :, :], Dx[:, :, :], ACT.Exp, scale=-DEC)
                    go(eg[:, :], gm[:, :], ACT.Exp, scale=-DEC)
                    wait(act, T, "kss", t)
                    go(rs[:, :, :], chan(B[3]), ACT.Ln, bias=eps12[:, :])
                    wait(act, A, "kln", t)
                    go(rs[:, :, :], rs[:, :, :], ACT.Exp, scale=-0.5)
                    wait(act, T, "flip", t)
                    wait(act, V, "bv", t - 1)
                    go(f3(v[0:n, :, :]), B[5][0:n, 0:W_C], ACT.Copy)
                    go(f3(bn[0:n, :, :]), B[6][0:n, 0:W_C], ACT.Copy)
                    go(f3(kn[0:n, :, :]), B[7][0:n, 0:W_C], ACT.Copy)
                    inv.act(act, T, A, t, B)
                    wait(act, T, "RH", t)
                    if sample:
                        wait(act, V, "r0", t)
                        go(f3(rhs[0:n, :, :]), f3(rhs[0:n, :, :]), ACT.Copy, scale=-1.0)
                    else:
                        for hh in range(2):
                            last = act.activation(rhs[0:n, hh::2, :], par(6, hh), ACT.Copy, scale=-1.0)
                        last.then_inc(A.sem, 1)
                    wait(act, T, "SA", t)
                    go(f3(sa[0:n, :, :]), B[0][0:n, 0:W_C], ACT.Copy)
                    wait(act, V, "ov", t)
                    go(ov[0:n, :], ov[0:n, :], ACT.Ln, scale=1.0 / HD, bias=eps_gn[0:n, :])
                    wait(act, A, "oln", t)
                    go(ov[0:n, :], ov[0:n, :], ACT.Exp, scale=-0.5)
                over_tiles(act, sample, body)

            @block.vector
            def _(dve):
                credit(dve, V)
                dve.wait_ge(cleared, 2)

                def body(t):
                    def tt(out, a, b, op):
                        dve.tensor_tensor(out, a, b, op).then_inc(V.sem, 1)

                    def ts(out, a, s1, s2, op0, op1=None):
                        (dve.tensor_scalar(out, a, s1, s2, op0, op1) if op1 else
                         dve.tensor_scalar(out, a, s1, s2, op0)).then_inc(V.sem, 1)

                    def stt(out, a, s, b, op0, op1):
                        dve.scalar_tensor_tensor(out, a, s, b, op0, op1).then_inc(V.sem, 1)

                    def own(name):
                        wait(dve, V, name, t)
                    wait(dve, A, "e1", t)
                    ts(th[:, :], th[:, :], 1.0, None, ALU.add)
                    own("th1")
                    dve.reciprocal(th[:, :], th[:, :]).then_inc(V.sem, 1)
                    own("th2")
                    ts(th[:, :], th[:, :], 2.0, -1.0, ALU.mult, ALU.add)
                    wait(dve, A, "e2", t)
                    ts(sg[:, :], sg[:, :], 1.0, None, ALU.add)
                    own("sg1")
                    dve.reciprocal(sg[:, :], sg[:, :]).then_inc(V.sem, 1)
                    tt(kx[:, :, :], c[:, 3:6, :], bc(k_k[:, :], n), ALU.mult)
                    own("kx")
                    tt(ksq[:, :, :], kx[:, :, :], kx[:, :, :], ALU.mult)
                    wait(dve, A, "ea", t)
                    ts(sig[:, :, :, :], sig[:, :, :, :], 1.0, None, ALU.add)
                    own("s1")
                    dve.reciprocal(sig[:, :, :, :], sig[:, :, :, :]).then_inc(V.sem, 1)
                    own("s2")
                    for j in range(3):
                        last = dve.tensor_tensor_scan(G_[:, j, :], scan[:, 0:n], sig[:, 0, j, :], 0.0,
                                                      ALU.mult, ALU.add)
                    last.then_inc(V.sem, 1)
                    own("scan")
                    if sample:
                        ts(gm[:, :], G_[:, :, 0], 0.0, None, ALU.mult)
                    else:
                        dve.tensor_copy(gm[:, :], G_[:, :, n // 2 - 1]).then_inc(V.sem, 1)
                    own("gm")
                    tt(G_[:, :, :], G_[:, :, :], bc(gm[:, :], n), ALU.subtract)
                    own("D")
                    tt(Dx[:, :, :], G_[:, :, :], sig[:, 0, :, :], ALU.subtract)
                    wait(dve, A, "krs", t)
                    tt(kk[:, :, :], kx[:, :, :], rs[:, :, :], ALU.mult)
                    stt(kp[:, :, :], sig[:, 1, :, :], -1.0, bc(k_a[:, :], n), ALU.add, ALU.mult)
                    own("kp1")
                    stt(kp[:, :, :], kp[:, :, :], 1.0, c[:, 3:6, :], ALU.add, ALU.mult)
                    own("kp2")
                    tt(bo[:, :, :], kp[:, :, :], c[:, 0:3, :], ALU.mult)
                    own("bo1")
                    tt(bo[:, :, :], bo[:, :, :], bc(r_k[:, :], n), ALU.mult)
                    tt(KR[:, :, 0, :], kk[:, :, :], ex[:, :, :], ALU.mult)
                    tt(KR[:, :, 1, :], c[:, 0:3, :], em[:, :, :], ALU.mult)
                    tt(Bt[:, :, :], kk[:, :, :], sig[:, 1, :, :], ALU.mult)
                    own("B1")
                    tt(Bt[:, :, :], Bt[:, :, :], ep[:, :, :], ALU.mult)
                    tt(Kt[:, :, :], kp[:, :, :], ep[:, :, :], ALU.mult)
                    wait(dve, T, "bs", t)
                    dve.tensor_copy(bs[0:n, :], B[4][0:n, 0:6]).then_inc(V.sem, 1)
                    for name, dst, b0 in (("b", APb, 0), ("k", APk, 4)):
                        for j, hs in enumerate(HEADS_OF_BANK):
                            wait(dve, T, f"{name}{j}", t)
                            dve.memset(tick[:, b0 + j:b0 + j + 1], 0.0)
                            nh = len(hs)
                            pair = lambda x: x.rearrange("p (h x) -> p h x", h=nh)
                            dve.copy_predicated(dst[0:n, hs[0]:hs[-1] + 1:2, :, :].rearrange("p h a n -> p h (a n)"),
                                                pair(mask2[0:n, 0:nh * 2 * n].bitcast(I32)),
                                                pair(B[b0 + j][0:n, 0:nh * 2 * n])).then_inc(V.sem, 1)
                    inv.dve_first(dve, V, Gp, t)
                    inv.dve(dve, T, V, t, B)
                    if sample:
                        for i in XS:
                            wait(dve, T, f"X{i}", t)
                            if i:
                                own(f"xr{i - 1}")
                            tt(xm[:, :, :], B[6 + i % 2][0:n, :].rearrange("p (b d) -> p b d", d=HD),
                               bc(seq[0:n, :], HD), ALU.mult)
                            own(f"xm{i}")
                            dve.tensor_reduce((ks, qs)[i // 6][:, i % 6, :], xm[:, :, :].rearrange("p b d -> p d b"),
                                              AX.X, ALU.add).then_inc(V.sem, 1)
                        wait(dve, T, "RH", t)
                        own("xr11")
                        for hh in range(2):
                            last = dve.tensor_tensor(rhs[0:n, hh::2, :], par(6, hh), ks[:, hh::2, :], ALU.add)
                        last.then_inc(V.sem, 1)
                        wait(dve, T, "O", t)
                        for hh in range(2):
                            last = dve.tensor_tensor(o[0:n, hh::2, :], par(4, hh), qs[:, hh::2, :], ALU.add)
                        last.then_inc(V.sem, 1)
                        for h in range(6):
                            if h >= 2:
                                wait(dve, T, f"U{h - 2}", t)
                            wait(dve, A, "sa", t)
                            dve.tensor_tensor(vx[:, h % 2, 0, :, :], mid(sa[0:n, h, :], NB), bc(seq[0:n, :], HD), ALU.mult)
                            tt(vx[:, h % 2, 1, :, :], mid(v[0:n, h, :], NB), bc(seq[0:n, :], HD), ALU.mult)
                            if h >= 1:
                                add_state(t, h - 1)
                        add_state(t, 5)
                        own("us5")
                        for p in range(3):
                            last = dve.tensor_tensor(S[:, :, p, :], S[:, :, p, :], bc(em[:, p, NQ - 1:n:NQ], HD), ALU.mult)
                        last.then_inc(V.sem, 1)
                    else:
                        wait(dve, V, "us", t - 1)
                        wait(dve, A, "eg", t)
                        tt(Sh[:, :, :], S[:, :, :], bc(eg[:, :], HD), ALU.mult)
                        wait(dve, T, "O", t)
                        for hh in range(2):
                            last = dve.tensor_copy(o[0:n, hh::2, :], par(4, hh))
                        last.then_inc(V.sem, 1)
                        wait(dve, T, "dS", t)
                        own("Sh")
                        for hh in range(2):
                            last = dve.tensor_tensor(
                                Sh[half(hh), :, :], Sh[half(hh), :, :],
                                B[2][half(hh), 0:W_A].rearrange("p (c d) -> p c d", d=P)[:, :, HD * hh:HD * hh + HD],
                                ALU.add)
                        last.then_inc(V.sem, 1)
                        own("us1")
                        tt(S[:, :, :], Sh[:, :, :], bc(em[:, :, n - 1], HD), ALU.mult)
                    own("o1")
                    dve.tensor_reduce(om[0:n, :], o[0:n, :, :], AX.X, ALU.add).then_inc(V.sem, 1)
                    own("om")
                    ts(om[0:n, :], om[0:n, :], 1.0 / HD, None, ALU.mult)
                    own("omn")
                    tt(o[0:n, :, :], o[0:n, :, :], bc(om[0:n, :], HD), ALU.subtract)
                    own("oc")
                    tt(osq[0:n, :, :], o[0:n, :, :], o[0:n, :, :], ALU.mult)
                    own("osq")
                    dve.tensor_reduce(ov[0:n, :], osq[0:n, :, :], AX.X, ALU.add).then_inc(V.sem, 1)
                    wait(dve, A, "ors", t)
                    tt(o[0:n, :, :], o[0:n, :, :], bc(ov[0:n, :], HD), ALU.mult)
                    own("on")
                    tt(f3(o[0:n, :, :]), f3(o[0:n, :, :]), lnw[0:n, :], ALU.mult)
                    own("ow")
                    tt(f3(o[0:n, :, :]), f3(o[0:n, :, :]), lnb[0:n, :], ALU.add)
                    own("bs")
                    wait(dve, A, "v", t)
                    tt(osq[0:n, :, :], v[0:n, :, :], bc(bs[0:n, :], HD), ALU.mult)
                    own("bv")
                    tt(o[0:n, :, :], o[0:n, :, :], osq[0:n, :, :], ALU.add)
                    own("obv")
                    if not sample:
                        dve.wait_ge(stored, t * 16 + 16)
                    tt(res[0:n, :, :], o[0:n, :, :], gate[0:n, :, :], ALU.mult)

                def add_state(t, h):
                    wait(dve, T, f"U{h}", t)
                    dve.tensor_tensor(S[half(h), :, h // 2, :], S[half(h), :, h // 2, :],
                                      B[2 + h % 2][half(h), :].rearrange("p (b d) -> p b d", d=HD), ALU.add)\
                       .then_inc(V.sem, 1)
                over_tiles(dve, sample, body)


def build(nc, ins, outs, upto=99):
    pr = Prog(nc, ins, outs)
    pr.cols = nc.dram_tensor("cols_t", [N_BLOCKS, P, TOK], F32).ap()
    pr.o_raw = nc.dram_tensor("o_raw", [TOK, D], F32).ap()
    pr.x1 = nc.dram_tensor("x1", [TOK, D], F32).ap()
    pr.x2 = nc.dram_tensor("x2", [TOK, D], F32).ap()
    pr.act_t = nc.dram_tensor("act_t", [FB, P, TOK], F32).ap()
    pr.pk, pr.pv = (outs[n][0, 0].rearrange("t h d -> t (h d)") for n in (2, 3))
    pr.sk, pr.sv = (outs[n][0].rearrange("b q h d -> (b q) (h d)") for n in (11, 12))
    with Stage(nc) as st:
        pr.ones = st.sb("ones", [P, P])
        pr.ident = st.sb("ident", [P, P])
        pr.eps = st.sb("eps", [P, 1])
        hT = st.sb("hT", [P, KD, TOK])
        g_mix, g_mem, g_ffn, g_kv = (st.sb(n, [P, KD]) for n in ("g_mix", "g_mem", "g_ffn", "g_kv"))
        taps = st.sb("taps", [P, 9, 4])
        mu = st.sb("mu", [P, 11, 1])
        gdn_old = st.sb("gdn_old", [P, 9, NB * 3])
        gdn_new = st.sb("gdn_new", [P, 9, (NB + 1) * 3])
        rw_old = st.sb("rw_old", [P, 11, NB])
        rw_new = st.sb("rw_new", [P, 11, NB + 1])
        vec = lambda a: a.rearrange("l (c p) -> p (l c)", p=P)
        prologue = Stage(nc).__enter__()
        old_a = prologue.sb("old_a", [NB * 3, 3 * W_A])
        old_c = prologue.sb("old_c", [NB, C_COLS])
        pr.const_loads = [
            (pr.ident[:, :], ins["c_ident"]), (pr.eps[:, :], ins["c_eps"]), (pr.ones[:, :], ins["c_ones"]),
            (g_mix[:, :], vec(ins["norm_mix"])), (g_mem[:, :], vec(ins["norm_mem"])),
            (g_ffn[:, :], vec(ins["norm_ffn"])), (g_kv[:, :], vec(ins["norm_mem_kv"])),
            (mu[:, :, 0], vec(ins["rw_mu"]))]
        pr.const_loads += [(taps[:, :, j], ins["gdn_conv_w"][0, j].rearrange("(c p) -> p c", p=P)) for j in range(4)]
        pr.const_loads += [(old_a[:, :], ins["state_gdn_conv"][0].rearrange("b j c -> (b j) c")),
                           (old_c[:, :], ins["state_rwkv_shift"][0])]
        load_constants(nc, pr)
        flip_blocks(nc, pr, [(old_a[:, c * P:(c + 1) * P], gdn_old[:, c, :]) for c in range(9)]
                    + [(old_c[:, c * P:(c + 1) * P], rw_old[:, c, :]) for c in range(11)])
        prologue.__exit__(None, None, None)

        def x_rows(t, n):
            return rows(ins["x_prompt"][0], t, n) if n == P else ins["x_sample"].rearrange("b q d -> (b q) d")
        norm_transpose(nc, pr, x_rows, g_mix, hT)
        project(nc, pr, hT, 9, 0, B_QKV, "conv", halo=3, taps=taps, state_in=gdn_old, saved=gdn_new)
        project(nc, pr, hT, 3, 3 * W_A, B_Z, "silu")
        project(nc, pr, hT, 6, A_COLS, B_DIFF, "plain")
        project(nc, pr, hT, 11, A_COLS + B_COLS, B_RWKV, "shift", halo=1, taps=mu, state_in=rw_old, saved=rw_new)
        project(nc, pr, hT, 1, 4 * W_A, B_BETA, "plain", m=2 * H_A)
        with Stage(nc) as ep:
            a_rows = ep.sb("a_rows", [3 * (NB + 1), 3 * W_A])
            c_rows = ep.sb("c_rows", [NB + 1, C_COLS])
            flip_blocks(nc, pr, [(gdn_new[:, c, :], a_rows[:, c * P:(c + 1) * P]) for c in range(9)]
                        + [(rw_new[:, c, :], c_rows[:, c * P:(c + 1) * P]) for c in range(11)])
            copy_in(nc, [(outs[4][0, 0], a_rows[0:3, :]),
                         (outs[13][0].rearrange("b j c -> (b j) c"), a_rows[3:, :]),
                         (outs[6][0], c_rows[0:1, :]), (outs[15][0], c_rows[1:, :])])
        if upto <= 1:
            return
        diff_rows(nc, pr, lambda t, n: rows(pr.pk, t, n) if n == P else pr.sk,
                  lambda t, n: rows(pr.pv, t, n) if n == P else pr.sv)
        with Stage(nc) as ds:
            causal = ds.sb("causal", [P, 4, 512])
            lam4 = ds.sb("lam4", [P, 4, DB])
            new_mask = ds.sb("new_mask", [P, NQ])
            sel0, sel1 = ds.sb("sel0", [32, 16]), ds.sb("sel1", [32, 16])
            selm = ds.sb("selm", [32, 16])
            prod, dots, neg_lam = ds.sb("prod", [P, 2, DB]), ds.sb("dots", [P, 2]), ds.sb("neg_lam", [P, 1])
            row = lambda a, n: a.broadcast_to([n, a.shape[1]])
            copy_in(nc, [(causal[:, :, :], ins["c_causal"]), (new_mask[:, :], ins["c_new"][:, 0, :]),
                         (sel0[:, :], ins["c_sel0"]), (sel1[:, :], ins["c_sel1"])]
                    + [(lam4[:, j, :], row(ins[n], P)) for j, n in
                       enumerate(("diff_lq1", "diff_lk1", "diff_lq2", "diff_lk2"))])
            with Stage(nc) as ls:
                step, exped = ls.sem("step"), ls.sem("exp")
                with nc.Block() as block:
                    @block.vector
                    def _(dve):
                        l2 = lam4[:, :, :].rearrange("p (a b) d -> p a b d", b=2)
                        dve.tensor_tensor(prod[:, :, :], l2[:, :, 0, :], l2[:, :, 1, :], ALU.mult).then_inc(step, 1)
                        dve.wait_ge(step, 1)
                        dve.tensor_reduce(dots[:, :], prod[:, :, :], AX.X, ALU.add).then_inc(step, 1)
                        dve.wait_ge(exped, 1)
                        dve.tensor_tensor(neg_lam[:, :], dots[:, 1:2], dots[:, 0:1], ALU.subtract).then_inc(step, 1)
                        dve.wait_ge(step, 3)
                        dve.tensor_scalar(neg_lam[:, :], neg_lam[:, :], -LAM_INIT, None, ALU.add).then_inc(step, 1)
                        dve.wait_ge(step, 4)
                        dve.scalar_tensor_tensor(selm[:, :], sel1[:, :], neg_lam[0:32, 0:1], sel0[:, :],
                                                 ALU.mult, ALU.add).then_inc(step, 1)

                    @block.scalar
                    def _(act):
                        act.wait_ge(step, 2)
                        act.activation(dots[:, :], dots[:, :], ACT.Exp).then_inc(exped, 1)
            diff_prompt(nc, pr, pr.pv, causal, neg_lam)
            diff_paged(nc, pr, pr.sk, pr.sv, selm, neg_lam, new_mask)
        if upto <= 2:
            return
        with Stage(nc) as ms:
            sb = ms.sb
            levels = sb("levels", [P, 7, P])
            strict, incl, quad, qstrict, qincl = (sb(x, [P, P]) for x in ("strict", "incl", "quad", "qstrict", "qincl"))
            seq = sb("seq", [P, NB])
            a_log, dt_b = sb("a_log", [P, 6]), sb("dt_b", [P, 6])
            norm_g = sb("norm_g", [P, HD])
            S_p, S_s = sb("S_p", [P, 3, HD]), sb("S_s", [P, NB, 3, HD])
            pairs = lambda a: a.rearrange("(c two) k v -> two k c v", two=2)
            loads = [(levels[:, :, :], ins["c_levels"]), (strict[:, :], ins["c_strict"]), (incl[:, :], ins["c_incl"]),
                     (quad[:, :], ins["c_quad"]), (qstrict[:, :], ins["c_quad_strict"]),
                     (qincl[:, :], ins["c_quad_incl"]), (seq[:, :], ins["c_seq"]), (a_log[:, :], row(ins["gdn_a_log"], P)),
                     (dt_b[:, :], row(ins["gdn_dt_bias"], P)), (norm_g[:, :], row(ins["gdn_norm"], P))]
            loads += [(S_s[half(hh), b, :, :], pairs(ins["state_gdn"][0, b])[hh]) for b in range(NB) for hh in range(2)]
            copy_in(nc, loads)
            with Stage(nc) as es:
                e, z = es.sem("e"), es.sem("z")
                with nc.Block() as block:
                    @block.scalar
                    def _(act):
                        act.activation(a_log[:, :], a_log[:, :], ACT.Exp).then_inc(e, 1)

                    @block.vector
                    def _(dve):
                        dve.memset(S_p[:, :, :], 0.0).then_inc(z, 1)
                        dve.wait_ge(e, 1)
                        dve.tensor_scalar(a_log[:, :], a_log[:, :], -1.0, None, ALU.mult).then_inc(z, 1)
            gdn(nc, pr, S_p, False, (pr.ones, strict, incl, levels, seq, a_log, dt_b, norm_g))
            gdn(nc, pr, S_s, True, (quad, qstrict, qincl, levels, seq, a_log, dt_b, norm_g))
            copy_in(nc, [(pairs(outs[5][0, 0])[hh], S_p[half(hh), :, :]) for hh in range(2)]
                    + [(pairs(outs[14][0, b])[hh], S_s[half(hh), b, :, :]) for b in range(NB) for hh in range(2)])
            if upto <= 3:
                return
            mask2p, mask2s = sb("mask2p", [P, 4 * P]), sb("mask2s", [P, 4 * NS])
            scan_p, scan_s = sb("scan_p", [P, P]), sb("scan_s", [P, NS])
            ones_half = sb("ones_half", [P, P])
            w2a2, g2 = sb("w2a2", [P, W_C]), sb("g2", [P, W_C])
            nw0, na0, k_k, k_a, r_k = (sb(x, [P, 3]) for x in ("nw0", "na0", "k_k", "k_a", "r_k"))
            lnw, lnb = sb("lnw", [P, W_C]), sb("lnb", [P, W_C])
            eps12, eps_gn = sb("eps12", [P, 1]), sb("eps_gn", [P, 1])
            rows_s = sb("rows_s", [HD, NB, 6, HD])
            rows_o = sb("rows_o", [HD, NB + 1, 3, P])
            copy_in(nc, [
                (mask2p[:, :], ins["c_mask2p"]), (mask2s[:, :], ins["c_mask2s"]), (scan_p[:, :], ins["c_ones"]),
                (scan_s[:, :], ins["c_scan"]), (ones_half[:, :], ins["c_half"]), (w2a2[0:64, :], ins["rw_w2"][0]),
                (w2a2[64:P, :], ins["rw_a2"][0]), (g2[:, :], ins["rw_g2"][0]), (nw0[:, :], vec(ins["rw_w0"])),
                (na0[:, :], vec(ins["rw_a0"])), (k_k[:, :], vec(ins["rw_k_k"])), (k_a[:, :], vec(ins["rw_k_a"])),
                (r_k[:, :], vec(ins["rw_r_k"].rearrange("l h d -> l (h d)"))), (lnw[:, :], row(ins["rw_lnx_w"], P)),
                (lnb[:, :], row(ins["rw_lnx_b"], P)), (eps12[:, :], ins["c_eps12"]), (eps_gn[:, :], ins["c_eps_gn"])]
                + [(rows_s[:, b, :, :], ins["state_rwkv"][0, b].rearrange("h v k -> v h k")) for b in range(NB)])
            with Stage(nc) as es:
                z = es.sem("z")
                with nc.Block() as block:
                    @block.vector
                    def _(dve):
                        dve.memset(S_p[:, :, :], 0.0).then_inc(z, 1)
                        dve.tensor_scalar(nw0[:, :], nw0[:, :], -1.0, None, ALU.mult).then_inc(z, 1)
                        dve.tensor_scalar(na0[:, :], na0[:, :], -1.0, None, ALU.mult).then_inc(z, 1)
            flip_blocks(nc, pr, [(rows_s[:, b, 2 * p:2 * p + 2, :].rearrange("v h k -> v (h k)"), S_s[:, b, p, :])
                                 for b in range(NB) for p in range(3)])
            common = (ones_half, w2a2, g2, nw0, na0, k_k, k_a, r_k, lnw, lnb, eps12, eps_gn)
            rwkv(nc, pr, S_p, False, (mask2p, levels, seq, scan_p) + common)
            rwkv(nc, pr, S_s, True, (mask2s, levels, seq, scan_s) + common)
            flip_blocks(nc, pr, [(S_p[:, p, :], rows_o[:, NB, p, :]) for p in range(3)]
                        + [(S_s[:, b, p, :], rows_o[:, b, p, :]) for b in range(NB) for p in range(3)])
            copy_in(nc, [((outs[16][0, b] if b < NB else outs[7][0, 0]).rearrange("h v k -> v h k"),
                          rows_o[:, b, :, :].rearrange("v c (two k) -> v (c two) k", two=2)) for b in range(NB + 1)])
        if upto <= 4:
            return
        with Stage(nc) as ts:
            subln = ts.sb("subln", [P, HD])
            copy_in(nc, [(subln[:, :], row(ins["diff_subln"], P))])
            mix_out(nc, pr, x_rows, g_mem, hT, subln)
        with Stage(nc) as ts:
            mK_T, mV = ts.sb("mK_T", [P, MH, MEM]), ts.sb("mV", [P, 2, MI])
            sample_o = ts.sb("sample_o", [P, MH, NS])
            with Stage(nc) as mt:
                mT = mt.sb("mT", [P, KD, MEM])
                norm_transpose(nc, pr, lambda t, n: rows(ins["mem_prompt"][0], t, n), g_kv, mT, n_tiles=2, tail=0)
                mem_project(nc, pr, mT, mK_T, mV, outs[9][0, 0].rearrange("m h d -> m (h d)"),
                            outs[10][0, 0].rearrange("m h d -> m (h d)"))
            mem_sample(nc, pr, hT, sample_o)
            mem_attention(nc, pr, hT, g_ffn, mK_T, mV, sample_o)
        if upto <= 5:
            return
        with Stage(nc) as ts:
            f_taps, f_bias = ts.sb("f_taps", [P, FB, 3]), ts.sb("f_bias", [P, FB])
            f_old, f_new = ts.sb("f_old", [P, FB, NB * 2]), ts.sb("f_new", [P, FB, (NB + 1) * 2])
            with Stage(nc) as pre:
                old = pre.sb("old", [NB * 2, D_FF])
                copy_in(nc, [(old[:, :], ins["state_ffn_conv"][0].rearrange("b j c -> (b j) c")),
                             (f_bias[:, :], vec(ins["ffn_conv_b"]))]
                        + [(f_taps[:, :, j], ins["ffn_conv_w"][0, j].rearrange("(c p) -> p c", p=P)) for j in range(3)])
                flip_blocks(nc, pr, [(old[:, c * P:(c + 1) * P], f_old[:, c, :]) for c in range(FB)])
            ffn_in(nc, pr, hT, f_taps, f_bias, f_old, f_new)
            with Stage(nc) as post:
                f_rows = post.sb("f_rows", [2 * (NB + 1), D_FF])
                flip_blocks(nc, pr, [(f_new[:, c, :], f_rows[:, c * P:(c + 1) * P]) for c in range(FB)])
                copy_in(nc, [(outs[8][0, 0], f_rows[0:2, :]),
                             (outs[17][0].rearrange("b j c -> (b j) c"), f_rows[2:, :])])
    with Stage(nc) as st:
        pr.eps = st.sb("eps", [P, 1])
        g_final = st.sb("g_final", [P, D])
        copy_in(nc, [(pr.eps[:, :], ins["c_eps"]),
                     (g_final[:, :], ins["norm_final"].rearrange("(a n) -> a n", a=1).broadcast_to([P, D]))])
        ffn_out(nc, pr, lambda t, n: rows(outs[0][0], t, n) if n == P else outs[1].rearrange("b q d -> (b q) d"), g_final)


_INS = ['x_prompt', 'x_sample', 'cache_diff_k', 'cache_diff_v', 'state_gdn_conv', 'state_gdn', 'state_rwkv_shift',
        'state_rwkv', 'state_ffn_conv', 'cache_mem_k', 'cache_mem_v', 'page_table', 'mem_prompt', 'norm_mix', 'w_in',
        'gdn_conv_w', 'gdn_a_log', 'gdn_dt_bias', 'gdn_norm', 'diff_lq1', 'diff_lk1', 'diff_lq2', 'diff_lk2',
        'diff_subln', 'rw_mu', 'rw_w0', 'rw_w2', 'rw_a0', 'rw_a2', 'rw_g2', 'rw_k_k', 'rw_k_a', 'rw_r_k', 'rw_lnx_w',
        'rw_lnx_b', 'w_out', 'norm_mem', 'norm_mem_kv', 'mem_wq', 'mem_wk', 'mem_wv', 'mem_wo', 'norm_ffn',
        'ffn_w_in', 'ffn_conv_w', 'ffn_conv_b', 'ffn_w_out', 'norm_final']
_OUTS = [(1, SEQ, D), (NB, NQ, D), (1, 1, SEQ, H_B, HD), (1, 1, SEQ, H_B, HD), (1, 1, 3, 3 * W_A),
         (1, 1, H_A, HD, HD), (1, 1, C_COLS), (1, 1, H_C, HD, HD), (1, 1, 2, D_FF), (1, 1, MEM, MH, MHD),
         (1, 1, MEM, MH, MHD), (1, NB, NQ, H_B, HD), (1, NB, NQ, H_B, HD), (1, NB, 3, 3 * W_A),
         (1, NB, H_A, HD, HD), (1, NB, C_COLS), (1, NB, H_C, HD, HD), (1, NB, 2, D_FF)]


def shape_constants():
    s, t = np.arange(P)[:, None], np.arange(P)[None, :]
    f = lambda a: np.ascontiguousarray(a, dtype=np.float32)
    levels = []
    for b in (1, 2, 4, 8, 16, 32, 64):
        levels.append((s // (2 * b) == t // (2 * b)) & ((s // b) % 2 == 0) & ((t // b) % 2 == 1))
    quad = s // NQ == t // NQ
    qi, ki = np.arange(P)[:, None, None], np.arange(512)[None, None, :]
    causal = np.where(ki <= qi + P * np.arange(4)[None, :, None], 0.0, NEG)
    new_ok = np.where(s[:, :, None] <= np.arange(NQ)[None, None, :], 0.0, NEG)
    rr, cc = np.arange(32)[:, None], np.arange(16)[None, :]
    same = (rr // 8 == cc // 4) & (rr % 4 == cc % 4)
    return dict(
        c_sel0=f(same & ((rr // 4) % 2 == 0)), c_sel1=f(same & ((rr // 4) % 2 == 1)),
        c_mask2p=f(np.tile(np.concatenate([s < t, s <= t], 1), (1, 2))),
        c_mask2s=f(np.tile(np.concatenate([(quad & (s < t))[:, :NS], (quad & (s <= t))[:, :NS]], 1), (1, 2))),
        c_scan=f(np.tile(np.arange(NS) % NQ != 0, (P, 1))), c_eps12=f(np.full((P, 1), 1e-12)),
        c_eps_gn=f(np.full((P, 1), 64e-5)),
        c_ident=f(np.eye(P)), c_eps=f(np.full((P, 1), EPS)), c_ones=f(np.ones((P, P))),
        c_half=f(s // HD == t // HD),
        c_levels=f(np.stack(levels, 1)),
        c_strict=f(s < t), c_incl=f(s <= t), c_quad=f(quad), c_quad_strict=f(quad & (s < t)),
        c_quad_incl=f(quad & (s <= t)), c_seq=f(s // NQ == np.arange(NB)[None, :]),
        c_causal=f(causal), c_new=f(new_ok[:, 0:1, :]))


def kernel(**inputs):
    import numpy as _np
    import concourse.bacc as _bacc
    from concourse import mybir as _mybir
    from concourse.bass_utils import run_bass_kernel_spmd as _run

    nc = _bacc.Bacc("TRN2", target_bir_lowering=False, num_devices=1)
    arrays, ins = {}, {}
    for name, a in [(n, inputs[n]) for n in _INS] + list(shape_constants().items()):
        a = _np.ascontiguousarray(a)
        arrays[f"in_{name}_dram"] = a
        ins[name] = nc.dram_tensor(f"in_{name}_dram", a.shape, _mybir.dt.from_np(a.dtype), kind="ExternalInput").ap()
    outs = [nc.dram_tensor(f"out_{i}_dram", shape, F32, kind="ExternalOutput").ap() for i, shape in enumerate(_OUTS)]
    build(nc, ins, outs)
    r = _run(nc, [arrays], core_ids=[0])
    return tuple(r.results[0][f"out_{i}_dram"] for i in range(len(_OUTS)))
```
